# Optimizing a Trainium2 kernel written in Bass

```python
import math
import jax, jax.numpy as jnp
from jax import lax
import numpy as np

D_MODEL = 1024
BATCH = 1
SEQ = 512
DEPTH = 1

FOX_HEADS = 4
FOX_HEAD_DIM = 64
FOX_WIDTH = FOX_HEADS * FOX_HEAD_DIM
Q_BLOCK = 128

GLA_HEADS = 4
GLA_DK = 32
GLA_DV = 64
GLA_KW = GLA_HEADS * GLA_DK
GLA_VW = GLA_HEADS * GLA_DV
GLA_RANK = 16
GLA_TAU = 16.0
GLA_CHUNK = 64

MOBA_HEADS = 4
MOBA_HEAD_DIM = 64
MOBA_WIDTH = MOBA_HEADS * MOBA_HEAD_DIM
MOBA_BLOCK = 256
MOBA_TOPK = 3

N_BRANCH = 3
BRANCH_WIDTH = 256

N_EXPERTS = 32
TOP_K = 4
D_EXPERT = D_MODEL
SWIGLU_LIMIT = 7.0
SWIGLU_ALPHA = 1.702
MOE_BLOCK = 128

ALPHA = (2 * DEPTH) ** 0.25
BETA = (8 * DEPTH) ** -0.25
LN_EPS = 1e-5
RMS_EPS = 1e-6

SPLIT_SIZES = (
    FOX_WIDTH, FOX_WIDTH, FOX_WIDTH, FOX_HEADS,
    GLA_KW, GLA_KW, GLA_VW, GLA_RANK, GLA_VW,
    MOBA_WIDTH, MOBA_WIDTH, MOBA_WIDTH,
    N_BRANCH * D_MODEL,
)
SPLIT_POINTS = tuple(int(p) for p in np.cumsum(SPLIT_SIZES)[:-1])
D_IN = sum(SPLIT_SIZES)

kernel_name = 'hybrid_fox_gla_moba_moe_deepnorm'

F32 = jnp.float32

def layer_norm(x, g, b):
    xf = x.astype(F32)
    mu = jnp.mean(xf, axis=-1, keepdims=True)
    var = jnp.mean(jnp.square(xf - mu), axis=-1, keepdims=True)
    return ((xf - mu) * lax.rsqrt(var + LN_EPS)).astype(x.dtype) * g + b

def head_rms_norm(o, g):
    B, S = o.shape[0], o.shape[1]
    of = o.astype(F32)
    of = of * lax.rsqrt(jnp.mean(of * of, axis=-1, keepdims=True) + RMS_EPS)
    return of.astype(o.dtype).reshape(B, S, -1) * g

def forgetting_attention(q, k, v, f_logit):
    B, S, H, Dh = q.shape
    c = jnp.cumsum(jax.nn.log_sigmoid(f_logit.astype(F32)), axis=1)
    cT = c.transpose(0, 2, 1)
    n_blk = S // Q_BLOCK
    qb = q.reshape(B, n_blk, Q_BLOCK, H, Dh).transpose(1, 0, 2, 3, 4)
    cb = c.reshape(B, n_blk, Q_BLOCK, H).transpose(1, 0, 2, 3)
    pos_k = jnp.arange(S)
    scale = Dh ** -0.5

    def block(args):
        i, q_i, c_i = args
        s = jnp.einsum('bqhd,bkhd->bhqk', q_i, k).astype(F32) * scale
        s = s + c_i.transpose(0, 2, 1)[..., None] - cT[:, :, None, :]
        pos_q = i * Q_BLOCK + jnp.arange(Q_BLOCK)
        s = jnp.where(pos_k[None, :] <= pos_q[:, None], s, -jnp.inf)
        p = jax.nn.softmax(s, axis=-1).astype(v.dtype)
        return jnp.einsum('bhqk,bkhd->bqhd', p, v)

    o = lax.map(block, (jnp.arange(n_blk), qb, cb))
    return o.transpose(1, 0, 2, 3, 4).reshape(B, S, H * Dh)

def gated_linear_attention(q, k, v, log_a):
    B, S, H, dk = q.shape
    dv = v.shape[-1]
    C = GLA_CHUNK
    n = S // C

    def to_chunks(t):
        return t.reshape(B, n, C, H, t.shape[-1]).transpose(1, 0, 3, 2, 4)

    qc, kc, vc, ac = to_chunks(q), to_chunks(k), to_chunks(v), to_chunks(log_a)
    causal = jnp.tril(jnp.ones((C, C), dtype=bool))
    scale = dk ** -0.5

    def step(state, inp):
        q_i, k_i, v_i, a_i = inp
        b = jnp.cumsum(a_i, axis=2)
        qf = q_i.astype(F32) * scale
        kf = k_i.astype(F32)
        vf = v_i.astype(F32)
        o_inter = jnp.einsum('bhck,bhkv->bhcv', qf * jnp.exp(b), state)
        diff = jnp.where(causal[..., None], b[:, :, :, None, :] - b[:, :, None, :, :], -jnp.inf)
        A = jnp.einsum('bhtk,bhsk,bhtsk->bhts', qf, kf, jnp.exp(diff))
        o_intra = jnp.einsum('bhts,bhsv->bhtv', A, vf)
        b_last = b[:, :, -1:, :]
        new_state = state * jnp.exp(b_last[:, :, 0, :])[..., None] + jnp.einsum(
            'bhck,bhcv->bhkv', kf * jnp.exp(b_last - b), vf)
        return new_state, o_inter + o_intra

    state0 = jnp.zeros((B, H, dk, dv), F32)
    _, o = lax.scan(step, state0, (qc, kc, vc, ac))
    return o.transpose(1, 0, 3, 2, 4).reshape(B, S, H, dv).astype(v.dtype)

def block_sparse_attention(q, k, v):
    B, S, H, Dh = q.shape
    L = MOBA_BLOCK
    Sp = -(-S // L) * L
    pad = ((0, 0), (0, Sp - S), (0, 0), (0, 0))
    nb = Sp // L
    n_gate = max(nb, MOBA_TOPK)
    kb = jnp.pad(k, pad).reshape(B, nb, L, H, Dh).transpose(0, 3, 1, 2, 4)
    vb = jnp.pad(v, pad).reshape(B, nb, L, H, Dh).transpose(0, 3, 1, 2, 4)
    k_mean = jnp.mean(kb.astype(F32), axis=3)
    k_mean = jnp.pad(k_mean, ((0, 0), (0, 0), (0, n_gate - nb), (0, 0)))
    n_q = S // Q_BLOCK
    qb = q.reshape(B, n_q, Q_BLOCK, H, Dh).transpose(1, 0, 2, 3, 4)
    scale = Dh ** -0.5
    bi = jnp.arange(B)[:, None, None, None]
    hi = jnp.arange(H)[None, None, :, None]
    slot = jnp.arange(MOBA_TOPK)
    blk_ids = jnp.arange(n_gate)

    def block(args):
        i, q_i = args
        pos_q = i * Q_BLOCK + jnp.arange(Q_BLOCK)
        own = (i * Q_BLOCK) // L
        gate = jnp.einsum('bqhd,bhnd->bqhn', q_i.astype(F32), k_mean)
        gate = jnp.where(blk_ids < own, gate, -jnp.inf)
        _, idx = lax.top_k(gate, MOBA_TOPK)
        idx = jnp.minimum(idx, nb - 1)
        valid = slot < own
        k_sel = kb[bi, hi, idx]
        v_sel = vb[bi, hi, idx]
        s_sel = jnp.einsum('bqhd,bqhnld->bqhnl', q_i, k_sel).astype(F32) * scale
        s_sel = jnp.where(valid[:, None], s_sel, -jnp.inf).reshape(B, Q_BLOCK, H, MOBA_TOPK * L)
        k_own = lax.dynamic_slice_in_dim(kb, own, 1, axis=2)[:, :, 0]
        v_own = lax.dynamic_slice_in_dim(vb, own, 1, axis=2)[:, :, 0]
        s_own = jnp.einsum('bqhd,bhld->bqhl', q_i, k_own).astype(F32) * scale
        pos_k = own * L + jnp.arange(L)
        s_own = jnp.where((pos_k[None, :] <= pos_q[:, None])[:, None, :], s_own, -jnp.inf)
        p = jax.nn.softmax(jnp.concatenate([s_sel, s_own], axis=-1), axis=-1).astype(v.dtype)
        p_sel = p[..., :MOBA_TOPK * L].reshape(B, Q_BLOCK, H, MOBA_TOPK, L)
        p_own = p[..., MOBA_TOPK * L:]
        return (jnp.einsum('bqhnl,bqhnld->bqhd', p_sel, v_sel)
                + jnp.einsum('bqhl,bhld->bqhd', p_own, v_own))

    o = lax.map(block, (jnp.arange(n_q), qb))
    return o.transpose(1, 0, 2, 3, 4).reshape(B, S, H * Dh)

def mixer(x, w_in, fox_fb, gla_a_up, gla_a_b, gla_norm_g, w_branch, w_out):
    B, S, _ = x.shape
    (fq, fk, fv, ff, gq, gk, gv, ga, gr, mq, mk, mv, gates) = jnp.split(
        x @ w_in, SPLIT_POINTS, axis=-1)

    def heads(t, h):
        return t.reshape(B, S, h, -1)

    y_fox = forgetting_attention(heads(fq, FOX_HEADS), heads(fk, FOX_HEADS), heads(fv, FOX_HEADS),
                                 ff + fox_fb)
    log_a = jax.nn.log_sigmoid((ga @ gla_a_up + gla_a_b).astype(F32)) / GLA_TAU
    o_gla = gated_linear_attention(heads(gq, GLA_HEADS), heads(gk, GLA_HEADS), heads(gv, GLA_HEADS),
                                   heads(log_a, GLA_HEADS))
    y_gla = head_rms_norm(o_gla, gla_norm_g) * jax.nn.silu(gr)
    y_moba = block_sparse_attention(heads(mq, MOBA_HEADS), heads(mk, MOBA_HEADS), heads(mv, MOBA_HEADS))
    ys = jnp.stack([y_fox, y_gla, y_moba], axis=2)
    up = jnp.einsum('bsnc,ncd->bsnd', ys, w_branch)
    g = jax.nn.sigmoid(gates.reshape(B, S, N_BRANCH, D_MODEL))
    merged = jnp.sum(g * up, axis=2)
    return merged @ w_out

def moe(x, w_router, b_router, w_gu, b_gu, w_dn, b_dn):
    B, S, D = x.shape
    T = B * S
    x2 = x.reshape(T, D)
    logits = (x2 @ w_router + b_router).astype(F32)
    top_v, top_i = lax.top_k(logits, TOP_K)
    gates = jax.nn.softmax(top_v, axis=-1).astype(x.dtype)
    n_assign = T * TOP_K
    flat_e = top_i.reshape(-1)
    flat_tok = jnp.repeat(jnp.arange(T, dtype=jnp.int32), TOP_K)
    order = jnp.argsort(flat_e)
    sorted_e = flat_e[order]
    sorted_tok = flat_tok[order]
    sorted_gate = gates.reshape(-1)[order]
    counts = jnp.bincount(flat_e, length=N_EXPERTS)
    padded = (counts + MOE_BLOCK - 1) // MOE_BLOCK * MOE_BLOCK
    pad_end = jnp.cumsum(padded)
    pad_start = pad_end - padded
    start = jnp.cumsum(counts) - counts
    dest = pad_start[sorted_e] + (jnp.arange(n_assign) - start[sorted_e])
    n_blocks = (n_assign + N_EXPERTS * (MOE_BLOCK - 1) + MOE_BLOCK - 1) // MOE_BLOCK
    buf_tok = jnp.zeros((n_blocks * MOE_BLOCK,), jnp.int32).at[dest].set(sorted_tok)
    block_expert = jnp.clip(jnp.searchsorted(pad_end, jnp.arange(n_blocks) * MOE_BLOCK, side='right'),
                            0, N_EXPERTS - 1)
    xin = x2[buf_tok].reshape(n_blocks, MOE_BLOCK, D)

    def expert_block(args):
        xb, e = args
        h = xb @ w_gu[e] + b_gu[e]
        gate = jnp.minimum(h[:, 0::2], SWIGLU_LIMIT)
        upv = jnp.clip(h[:, 1::2], -SWIGLU_LIMIT, SWIGLU_LIMIT)
        act = (upv + 1.0) * (gate * jax.nn.sigmoid(SWIGLU_ALPHA * gate))
        return act @ w_dn[e] + b_dn[e]

    yb = lax.map(expert_block, (xin, block_expert)).reshape(n_blocks * MOE_BLOCK, D)
    y_assign = yb[dest] * sorted_gate[:, None]
    out = jnp.zeros((T, D), x.dtype).at[sorted_tok].add(y_assign)
    return out.reshape(B, S, D)

def setup_inputs(seed: int = 0) -> dict:
    key = jax.random.key(seed)
    ks = jax.random.split(key, 20)
    nrm = jax.random.normal
    x = nrm(ks[0], (BATCH, SEQ, D_MODEL), F32)
    w_in = nrm(ks[1], (DEPTH, D_MODEL, D_IN), F32) * D_MODEL ** -0.5
    fox_fb = (jnp.linspace(1.0, 5.0, FOX_HEADS, dtype=F32)[None, :]
              + 0.01 * nrm(ks[2], (DEPTH, FOX_HEADS), F32))
    gla_a_up = nrm(ks[3], (DEPTH, GLA_RANK, GLA_KW), F32) * GLA_RANK ** -0.5
    gla_a_b = 0.01 * nrm(ks[4], (DEPTH, GLA_KW), F32)
    gla_norm_g = 1.0 + 0.01 * nrm(ks[5], (DEPTH, GLA_VW), F32)
    w_branch = nrm(ks[6], (DEPTH, N_BRANCH, BRANCH_WIDTH, D_MODEL), F32) * BRANCH_WIDTH ** -0.5
    w_out = nrm(ks[7], (DEPTH, D_MODEL, D_MODEL), F32) * (D_MODEL ** -0.5 * BETA)
    ln1_g = 1.0 + 0.01 * nrm(ks[8], (DEPTH, D_MODEL), F32)
    ln1_b = 0.01 * nrm(ks[9], (DEPTH, D_MODEL), F32)
    w_router = nrm(ks[10], (DEPTH, D_MODEL, N_EXPERTS), F32) * D_MODEL ** -0.5
    b_router = 0.01 * nrm(ks[11], (DEPTH, N_EXPERTS), F32)
    w_gu = nrm(ks[12], (DEPTH, N_EXPERTS, D_MODEL, 2 * D_EXPERT), F32) * D_MODEL ** -0.5
    b_gu = 0.01 * nrm(ks[13], (DEPTH, N_EXPERTS, 2 * D_EXPERT), F32)
    w_dn = nrm(ks[14], (DEPTH, N_EXPERTS, D_EXPERT, D_MODEL), F32) * (D_EXPERT ** -0.5 * BETA)
    b_dn = 0.01 * nrm(ks[15], (DEPTH, N_EXPERTS, D_MODEL), F32)
    ln2_g = 1.0 + 0.01 * nrm(ks[16], (DEPTH, D_MODEL), F32)
    ln2_b = 0.01 * nrm(ks[17], (DEPTH, D_MODEL), F32)
    return {'x': x, 'w_in': w_in, 'fox_fb': fox_fb, 'gla_a_up': gla_a_up, 'gla_a_b': gla_a_b,
            'gla_norm_g': gla_norm_g, 'w_branch': w_branch, 'w_out': w_out,
            'ln1_g': ln1_g, 'ln1_b': ln1_b, 'w_router': w_router, 'b_router': b_router,
            'w_gu': w_gu, 'b_gu': b_gu, 'w_dn': w_dn, 'b_dn': b_dn,
            'ln2_g': ln2_g, 'ln2_b': ln2_b}

def reference(x, w_in, fox_fb, gla_a_up, gla_a_b, gla_norm_g, w_branch, w_out,
              ln1_g, ln1_b, w_router, b_router, w_gu, b_gu, w_dn, b_dn, ln2_g, ln2_b):
    for l in range(DEPTH):
        m = mixer(x, w_in[l], fox_fb[l], gla_a_up[l], gla_a_b[l], gla_norm_g[l], w_branch[l], w_out[l])
        x = layer_norm(ALPHA * x + m, ln1_g[l], ln1_b[l])
        f = moe(x, w_router[l], b_router[l], w_gu[l], b_gu[l], w_dn[l], b_dn[l])
        x = layer_norm(ALPHA * x + f, ln2_g[l], ln2_b[l])
    return x


_drawn_inputs = setup_inputs


def setup_inputs(seed=0):
    import zlib

    import numpy as np

    out = dict(_drawn_inputs(seed))
    spreads = {}
    factors = {'gla_a_b': 8.0,
     'gla_norm_g': 21.475,
     'ln1_g': 2.894,
     'ln1_b': 2.685,
     'b_router': 3.495,
     'b_gu': 8.0,
     'b_dn': 35.331,
     'ln2_g': 32.614,
     'ln2_b': 32.828}
    for name, (base, spread) in spreads.items():
        noise = np.random.default_rng([zlib.crc32(name.encode()), seed]).standard_normal(out[name].shape)
        drawn = base * np.exp(spread * noise) if base else spread * noise
        out[name] = __import__('jax').numpy.asarray(drawn.astype(out[name].dtype))
    for name, factor in factors.items():
        out[name] = (out[name] * factor).astype(out[name].dtype)
    return out
```

```python
from contextlib import ExitStack

import concourse.bass as bass
from concourse import mybir

D = 1024
T = 512
P = 128
KT = D // P
TT = T // P
HEADS = 4
DH = 64
DK = 32
E = 32
TOPK = 4
NB = T // P
ALPHA = 2.0 ** 0.25
LN_EPS = 1e-5
RMS_EPS = 1e-6
TAU = 16.0
LIMIT = 7.0
SWIGLU = 1.702
NEG = -1e30
MAX_EXTRA = (T * TOPK) // (P + 1)

CW = 2048
N_MIX = 30
CPE = 12
RAW_MIX, SPLIT_MIX = 4, 2
RAW, SPLIT = 8, 4
UNROLL = 2
LOOK = SPLIT
POOL_CHUNKS = (5, 10)

SMALL, GQ, GK, FQ, FK, MQ, MK = 0, 1, 2, 3, 5, 7, 9
TOK = 11
GATE = 19
GATE_SLOTS = 12
W_GATES = [10 + g // 2 if g < 12 else 17 + (g - 12) // 2 if g < 18 else 21 + (g - 18) // 2 for g in range(24)]
W_UP = [16, 16, 20, 20, 24, 24, 25, 25]
W_OUT = 26
LEVELS = (64, 32, 16, 8, 4, 2, 1)


def chunk_of(mt):
    if mt == SMALL:
        return 0, 0
    if mt < TOK:
        return (mt + 1) // 2, (mt + 1) % 2
    return W_GATES[mt - GATE], (mt - GATE) % 2


EARLY = [("mt", 0), ("mt", 1), ("mt", 2), ("decay", 0), ("mt", 3), ("mt", 4), ("mt", 5), ("level", 0), ("mt", 6),
         ("level", 1), ("mt", 7), ("level", 2), ("mt", 8), ("level", 3), ("mt", 9), ("level", 4), ("mt", 10),
         ("level", 5), ("tok", 0), ("level", 6), ("tok", 1), ("level", 7), ("tok", 2), ("carry", 0), ("tok", 3),
         ("carry", 1), ("carry", 2), ("carry", 3)]
UNITS = 2 * HEADS * TT
A_STEPS = UNITS + 2
LATE = [("up", 0), ("up", 1)] + [("gate", g) for g in range(12, 18)] + [("up", 2), ("up", 3)] + \
       [("gate", g) for g in range(18, 24)] + [("up", d) for d in (4, 5, 6, 7)]


def unit(u):
    branch, h, qt = u // (HEADS * TT), (u // TT) % HEADS, u % TT
    return branch, h, qt


def build_kernel(nc, xT, x, wmix, wexp, a_up, a_b, fb, norm_g, ln1_g, ln1_b, w_router, b_router, b_moe, ln2_g, ln2_b,
                 cf, cb, masks, extra_c, out):
    F32, F32R, BF16 = mybir.dt.float32, mybir.dt.float32r, mybir.dt.bfloat16
    I32, U32, U8 = mybir.dt.int32, mybir.dt.uint32, mybir.dt.uint8
    ALU = mybir.AluOpType
    ACT = mybir.ActivationFunctionType
    AX = mybir.AxisListType

    ctx = ExitStack()
    with ctx:
        BASE = -(-nc.sbuf_base // 64) * 64
        A0 = BASE
        B0 = A0 + RAW * 8192
        C0 = B0 + SPLIT * 16384
        D0 = C0 + 32768
        D1 = D0 + 18432
        K0 = D1 + 24576

        def at(name, shape, dt, offset):
            return nc.alloc_sbuf_tensor_at(name, shape, dt, offset=offset)

        small_at = [K0]

        def small(name, shape, dt):
            size = {F32: 4, I32: 4, U32: 4, BF16: 2, U8: 1}[dt]
            for n in shape[1:]:
                size *= n
            t = at(name, shape, dt, small_at[0])
            small_at[0] += -(-size // 32) * 32
            return t

        raw = [at(f"raw{s}", [P, CW], F32, A0 + 8192 * s) for s in range(RAW)]
        w_hi = [at(f"w_hi{s}", [P, CW], F32R, B0 + 16384 * s) for s in range(SPLIT)]
        w_lo = [at(f"w_lo{s}", [P, CW], F32R, B0 + 16384 * s + 8192) for s in range(SPLIT)]
        xT_hi = at("xT_hi", [P, KT, T], F32R, B0 + 32768)
        xT_lo = at("xT_lo", [P, KT, T], F32R, B0 + 49152)
        x1 = at("x1", [P, TT, D], F32, B0 + 32768)
        x1T = at("x1T", [P, KT, T], F32, B0 + 49152)
        G0 = A0 + 32768
        scoreT = at("scoreT", [P, HEADS, T], F32, G0)
        decay = at("decay", [P, T], F32, G0 + 8192)
        ratio = at("ratio", [P, T], F32, G0 + 10240)
        q_dec = [at(f"q_dec{i}", [P, T], F32, G0 + 12288 + 2048 * i) for i in range(2)]
        k_dec = [at(f"k_dec{i}", [P, T], F32, G0 + 16384 + 2048 * i) for i in range(2)]
        squares = at("squares", [P, 4 * 256], F32, G0 + 16384)
        k_end = at("k_end", [P, T], F32, G0 + 20480)
        k_endT = at("k_endT", [P, T], F32, G0 + 22528)
        state = at("state", [P, 3, 256], F32, G0 + 24576)
        y_gla = at("y_gla", [P, TT, 256], F32, G0 + 27648)
        norm_gb = at("norm_gb", [P, 256], F32, G0 + 31744)
        log1p = at("log1p", [P, T], F32, G0 + 22528)
        f_raw = at("f_raw", [HEADS, T], F32, G0 + 27648)
        f_log = at("f_log", [HEADS, T], F32, G0 + 29696)
        f_cum = at("f_cum", [HEADS, T], F32, G0 + 24576)
        ga_sb = at("ga_sb", [16, T], F32, G0 + 20480)
        probs = [at(f"probs{i}", [P, T], F32, G0 + 2048 * i) for i in range(2)]
        probsT = [at(f"probsT{i}", [P, T], F32, G0 + 4096 + 2048 * i) for i in range(2)]
        mix_acc = [at(f"mix_acc{i}", [P, T], F32, G0 + 2048 * i) for i in range(2)]
        mix_tmp = [at(f"mix_tmp{i}", [P, T], F32, G0 + 4096 + 2048 * i) for i in range(2)]
        gates = at("gates", [P, GATE_SLOTS, T], F32, G0 + 8192)
        f_q = at("f_q", [P, HEADS, T], F32, C0)
        f_k = at("f_k", [P, HEADS, T], F32, C0 + 8192)
        m_q = at("m_q", [P, 2, T], F32, C0 + 16384)
        m_k = at("m_k", [P, 2, T], F32, C0 + 20480)
        g_q = at("g_q", [P, T], F32, C0 + 24576)
        g_k = at("g_k", [P, T], F32, C0 + 26624)
        level_mask = at("level_mask", [P, 8, P], U8, C0 + 28672)
        head_mask = at("head_mask", [P, 256], F32, C0 + 29696)
        merged_hi = at("merged_hi", [P, KT, T], F32R, C0)
        merged_lo = at("merged_lo", [P, KT, T], F32R, C0 + 16384)
        values = at("values", [P, TT, D], F32, D0)
        mask_in = at("mask_in", [P, 8, P], F32, D0)
        cst_b_in = at("cst_b_in", [P, 4 * P + E], F32, D0 + 4096)
        bias_f = at("bias_f", [96, 3 * D], F32, D0)
        bias3 = at("bias3", [96, 3 * D], BF16, D0 + 12288)
        xT_in = at("xT_in", [P, KT, T], F32, D1)
        yT_hi = at("yT_hi", [P, 6, T], F32R, D1)
        yT_lo = at("yT_lo", [P, 6, T], F32R, D1 + 12288)
        ln_g = at("ln_g", [P, D], F32, D1)
        ln_b = at("ln_b", [P, D], F32, D1 + 4096)
        x_tok = at("x_tok", [P, TT, D], F32, D1 + 8192)
        glu_g = at("glu_g", [P, 512], F32, C0)
        glu_u = at("glu_u", [P, 512], F32, C0 + 2048)
        glu_s = at("glu_s", [P, 512], F32, C0 + 4096)
        act = [at(f"act{h}", [P, 512], F32, C0 + 6144 + 2048 * h) for h in range(2)]
        y_sb = at("y_sb", [P, D], F32, C0 + 10240)
        x_rows = at("x_rows", [P, D], F32, C0 + 16384)
        xe_hi = at("xe_hi", [P, KT, P], F32R, C0 + 20480)
        xe_lo = at("xe_lo", [P, KT, P], F32R, C0 + 24576)
        aT_hi = [at(f"aT_hi{h}", [P, 4, P], F32R, D1 + 4096 * h) for h in range(2)]
        aT_lo = [at(f"aT_lo{h}", [P, 4, P], F32R, D1 + 4096 * h + 2048) for h in range(2)]
        y_rows = [at(f"y_rows{i}", [P, TOPK, D], F32, A0 + 16384 * i) for i in range(2)]
        x_end = at("x_end", [P, TT, D], F32, A0 + 32768)
        res = [at(f"res{i}", [P, D], F32, B0 + 4096 * i) for i in range(2)]
        ln_t = [at(f"ln_t{i}", [P, D], F32, B0 + 8192 + 4096 * i) for i in range(2)]
        ln2g = at("ln2g", [P, D], F32, D1 + 8192)
        ln2b = at("ln2b", [P, D], F32, D1 + 12288)


        cst = small("cst", [P, 3 * P + 16], F32)
        ident = cst[:, 0:P]
        iota = cst[:, P:2 * P]
        ones = cst[:, 2 * P:3 * P]
        row_id = cst[:, 3 * P:3 * P + 16]
        cst_b = small("cst_b", [P, 4 * P + E], BF16)
        ident_b = cst_b[:, 0:P]
        causal = cst_b[:, P:2 * P]
        before = cst_b[:, 2 * P:3 * P]
        ones_b = cst_b[:, 3 * P:4 * P]
        pick = cst_b[0:96, 4 * P:4 * P + E]
        a_up_sb = small("a_up_sb", [16, P], F32)
        a_b_sb = small("a_b_sb", [P, 1], F32)
        fb_sb = small("fb_sb", [HEADS, 1], F32)
        b_r = small("b_r", [P, E], F32)
        scatter_ix = small("scatter_ix", [P, P], I32)
        gather_ix = small("gather_ix", [P, P], I32)
        gix_now = small("gix_now", [P, 1], I32)
        six_now = small("six_now", [P, 1], I32)
        pool_idle = small("pool_idle", [P, 1], F32)
        gate_w = small("gate_w", [P, TT, TOPK], F32)
        counts = small("counts", [1, E], F32)
        n_extra = small("n_extra", [1, 1], I32)
        extra = small("extra", [1, 16], I32)
        stats = small("stats", [P, TT, 12], F32)
        mean_var = small("mean_var", [P, TT, 2], F32)
        std = small("std", [P, TT], F32)
        top_v = small("top_v", [P, TT, 8], F32)
        top_i = small("top_i", [P, TT, 8], U32)
        ix_f = small("ix_f", [P, TT, TOPK], F32)
        pos, blk, slot, col_f = (small(n, [P, TT * TOPK], F32) for n in ("pos", "blk", "slot", "col_f"))
        exp4 = small("exp4", [P, TT, TOPK], F32)
        exp_sum = small("exp_sum", [P, TT], F32)
        row_max = small("row_max", [P, 2], F32)
        row_sum = small("row_sum", [P, 2], F32)
        row_inv = small("row_inv", [P, 2], F32)
        rms = small("rms", [P, 4 * HEADS], F32)
        end_dec = small("end_dec", [P, TT], F32)
        assert small_at[0] <= nc.sbuf_usable_end, (small_at[0], nc.sbuf_usable_end)
        w_r = at("w_r", [P, KT, E], F32, C0 + 30720)
        onehot_s = at("onehot_s", [P, TT * TOPK, P], F32, D1)
        onehot_c = at("onehot_c", [P, TT * TOPK, P], F32, D1 + 8192)
        table = at("table", [P, P], F32, D0)
        wrap = at("wrap", [P, P], F32, D0 + 512)
        wrapped = at("wrapped", [P, P], F32, D0 + 1024)
        logits = at("logits", [P, TT, E], F32, D0 + 1536)
        hits = at("hits", [P, TT, E], BF16, D0 + 2048)
        junk = at("junk", [P, E], F32, D0 + 2304)
        over = at("over", [1, E], F32, D0 + 2560)
        chosen = at("chosen", [P, TT, TOPK, E], F32, D0 + 4096)
        places_of = at("places_of", [P, TT, TOPK, E], F32, D0 + 6144)
        extra_on = at("extra_on", [1, P], F32, D0)
        extra_sum = at("extra_sum", [1, P], F32, D0 + 512)
        extra_eq = at("extra_eq", [1, 16, P], F32, D0 + 1024)
        extra_f = at("extra_f", [1, 16], F32, D0 + 9216)
        extra_cst = at("extra_cst", [1, P + 16], F32, D0 + 9280)

        bank = [ctx.enter_context(nc.psum_tensor(f"bank{i}", [P, 512], F32)) for i in range(8)]
        x1_dram = nc.dram_tensor("x1_scratch", (T, D), F32, kind="Internal").ap()
        y_dram = nc.dram_tensor("y_scratch", (TOPK * T, D), F32, kind="Internal").ap()

        def sem(name):
            return ctx.enter_context(nc.semaphore(name))

        x_in = [sem("x_in0"), sem("x_in1")]
        cst_in, gla_in, crow_in, bias_in, tok_in, w_r_in, x1_out = (
            sem(n) for n in ("cst_in", "gla_in", "crow_in", "bias_in", "tok_in", "w_r_in", "x1_out"))
        mix_in = [sem(f"mix_in{s}") for s in range(RAW_MIX)]
        ln2_in, x_end_in, y_in, out_done = sem("ln2_in"), sem("x_end_in"), [sem("y_in0"), sem("y_in1")], [sem("out_done0"), sem("out_done1")]
        m_hi, m_lo, x_hi, x_lo = sem("m_hi"), sem("m_lo"), sem("x_hi"), sem("x_lo")
        used, first_tile, proj_read = sem("used"), sem("first_tile"), sem("proj_read")
        pool_ready = sem("pool_ready")
        decay_pre, log_ready, decay_ready, diff_ready, ratio_ready, qk_ready = (
            sem(n) for n in ("decay_pre", "log_ready", "decay_ready", "diff_ready", "ratio_ready", "qk_ready"))
        level_done, level_read, crow_ready = sem("level_done"), sem("level_read"), sem("crow_ready")
        carry_pe, carry_act, carry_dve = sem("carry_pe"), sem("carry_act"), sem("carry_dve")
        score_done, max_ready, exp_done, norm_done, pT_done, pT_read, pv_done = (sem(n) for n in (
            "score_done", "max_ready", "exp_done", "norm_done", "pT_done", "pT_read", "pv_done"))
        yT_hi_ready, yT_lo_ready = sem("yT_hi_ready"), sem("yT_lo_ready")
        gate_sig, up_done, up_read, merged_ready, merged_hi_ready, merged_lo_ready, bias_ready = (sem(n) for n in (
            "gate_sig", "up_done", "up_read", "merged_ready", "merged_hi_ready", "merged_lo_ready", "bias_ready"))
        var_ready, std_ready, scaled, x1_ready, x1T_done, x1T_read = (sem(n) for n in (
            "var_ready", "std_ready", "scaled", "x1_ready", "x1T_done", "x1T_read"))
        logit_done, top_ready, gate_exp, hits_ready, pos_done, onehot_ready, onehot_used, counted, route_ready = (
            sem(n) for n in ("logit_done", "top_ready", "gate_exp", "hits_ready", "pos_done", "onehot_ready", "onehot_used",
                             "counted", "route_ready"))
        dve_step, act_step = sem("dve_step"), sem("act_step")
        extra_in, extra_step, extra_ready = sem("extra_in"), sem("extra_step"), sem("extra_ready")
        end_step = sem("end_step")
        experts_done, end_first, end_sum, end_var, end_std, end_scaled, end_ready = (sem(n) for n in (
            "experts_done", "end_first", "end_sum", "end_var", "end_std", "end_scaled", "end_ready"))

        class Pass:

            def __init__(self, tag, slots, alone):
                self.alone, self.slots = alone, slots
                self.raw_in = [sem(f"{tag}_raw_in{s}") for s in range(slots)]
                self.hi, self.lo_dve, self.lo_pool, self.used = (
                    sem(f"{tag}_{n}") for n in ("hi", "lo_dve", "lo_pool", "used"))
                self.tr, self.tr_hi, self.tr_lo = sem(f"{tag}_tr"), sem(f"{tag}_tr_hi"), sem(f"{tag}_tr_lo")
                self.glu_read, self.sig, self.gated, self.act_ready = (
                    sem(f"{tag}_{n}") for n in ("glu_read", "sig", "gated", "act_ready"))
                self.y_copied, self.gathered, self.scattered = (
                    sem(f"{tag}_{n}") for n in ("y_copied", "gathered", "scattered"))
                self.gix, self.six = sem(f"{tag}_gix"), sem(f"{tag}_six")
                self.dve_chunks = [m for m in range(CPE) if alone or m not in POOL_CHUNKS]

            def wait_lo(self, eng, e, m):
                e, m = e + m // CPE, m % CPE
                if m in self.dve_chunks:
                    n = len(self.dve_chunks)
                    eng.wait_ge(self.lo_dve, e * n + (self.dve_chunks.index(m) + 1))
                else:
                    eng.wait_ge(self.lo_pool, e * len(POOL_CHUNKS) + (POOL_CHUNKS.index(m) + 1))

            def wait_raw(self, eng, e, p, m):
                if self.alone:
                    eng.wait_ge(self.raw_in[m % self.slots], (e * (CPE // self.slots) + m // self.slots + 1) * 16)
                else:
                    c = p * CPE + m
                    eng.wait_ge(self.raw_in[c % self.slots], ((e - p) * CPE // RAW + c // self.slots + 1) * 16)

            def raw(self, p, m):
                return raw[m % self.slots] if self.alone else raw[(p * CPE + m) % self.slots]

            def transposes(self, e, last):
                return (e * 4 + 2, e * 4 + 3) if self.alone or last else (e * 4 + 2, e * 4 + 4)

        first, more = Pass("first", RAW, False), Pass("more", SPLIT, True)
        block = ctx.enter_context(nc.Block())

        def linked(eng, s):
            count = [0]

            def link(ins):
                count[0] += 1
                ins.then_inc(s, 1)
                eng.wait_ge(s, count[0])
            return link

        def tile_done(mt):
            if TOK <= mt < GATE:
                return used, 8 if mt < TOK + TT else 10
            c, j = chunk_of(mt)
            if j == 0 and mt != SMALL:
                return first_tile, c if mt < TOK else 6 + (mt - GATE) // 2
            return used, c + 1

        def up_signal(i):
            return (used, W_UP[i // 3] + 1) if i % 6 == 5 else (up_done, i - i // 6 + 1)

        def freed(kind, n):
            if kind in ("mt", "gate"):
                c, j = chunk_of(n if kind == "mt" else GATE + n)
                return c if j == 1 or c == 0 else None
            if kind == "tok":
                return 6 + n
            if kind == "up":
                return W_UP[n] if n % 2 else None
            return W_OUT + n if kind == "out" else None

        def fill(s):
            return (s // 3, s % 3) if s < 36 else None

        FILL_STEPS = 36
        turns = E // UNROLL

        def passes(eng, body):
            for p in range(UNROLL):
                body(p, p, p == UNROLL - 1 and turns == 1)
            with eng.Fori(1, turns - 1) as i:
                for p in range(UNROLL):
                    body(i * UNROLL + p, p, False)
            for p in range(UNROLL):
                body(E - UNROLL + p, p, p == UNROLL - 1)

        @block.sync
        def _(sp):
            for h in range(2):
                sp.dma_start(xT_in[:, 4 * h:4 * h + 4, :], xT[:, 4 * h:4 * h + 4, :]).then_inc(x_in[h], 16)
            for c in range(N_MIX):
                s = c % RAW_MIX
                if c >= RAW_MIX:
                    sp.wait_ge(m_lo, c - RAW_MIX + 1)
                sp.dma_start(raw[s][:, :], wmix[c]).then_inc(mix_in[s], 16)
                if c == 1:
                    for to, src in ((cst[:, :], cf[:, 0:3 * P + 16]), (cst_b_in[:, :], cb)):
                        sp.dma_start(to, src).then_inc(cst_in, 16)
                    for to, src in ((a_up_sb[:, :], a_up), (a_b_sb[:, :], a_b), (fb_sb[:, :], fb),
                                    (mask_in[:, :, :], masks), (head_mask[:, :], cf[:, 3 * P + 16:5 * P + 16]),
                                    (norm_gb[:, :], norm_g.partition_broadcast(P))):
                        sp.dma_start(to, src).then_inc(gla_in, 16)
                if c == 19:
                    sp.wait_ge(pv_done, UNITS)
                    for q in range(3):
                        sp.dma_start(bias_f[32 * q:32 * q + 32, :], b_moe).then_inc(bias_in, 16)
            sp.wait_ge(used, W_UP[-1] + 1)
            for to, src in ((x_tok[:, :, :], x), (ln_g[:, :], ln1_g.partition_broadcast(P)),
                            (ln_b[:, :], ln1_b.partition_broadcast(P)), (b_r[:, :], b_router.partition_broadcast(P))):
                sp.dma_start(to, src).then_inc(tok_in, 16)
            sp.wait_ge(merged_lo_ready, KT)
            for c in (4, 5, 6, 7):
                sp.dma_start(raw[c][:, :], wexp[c * P:(c + 1) * P, :]).then_inc(first.raw_in[c], 16)
            sp.wait_ge(m_lo, N_MIX)
            for c in (0, 1, 2, 3):
                sp.dma_start(raw[c][:, :], wexp[c * P:(c + 1) * P, :]).then_inc(first.raw_in[c], 16)
            sp.wait_ge(used, N_MIX)
            sp.dma_start(w_r[:, :, :], w_router).then_inc(w_r_in, 16)
            for t in range(TT):
                sp.wait_ge(x1_ready, t + 1)
                sp.dma_start(x1_dram[t * P:(t + 1) * P, :], x1[:, t, :]).then_inc(x1_out, 16)
            for c in range(RAW, CPE * UNROLL):
                first.wait_lo(sp, 0, c - RAW)
                sp.dma_start(raw[c % RAW][:, :], wexp[c * P:(c + 1) * P, :]).then_inc(first.raw_in[c % RAW], 16)
            with sp.Fori(1, turns) as i:
                for c in range(CPE * UNROLL):
                    first.wait_lo(sp, i * UNROLL + (c - RAW) // CPE, (c - RAW) % CPE)
                    sp.dma_start(raw[c % RAW][:, :], wexp[bass.ds((i * (CPE * UNROLL) + c) * P, P), :])\
                      .then_inc(first.raw_in[c % RAW], 16)
            for to, src in ((ln2g[:, :], ln2_g), (ln2b[:, :], ln2_b)):
                sp.dma_start(to, src.partition_broadcast(P)).then_inc(ln2_in, 16)
            sp.wait_ge(route_ready, 2)
            n = sp.value_load(n_extra[0:1, 0:1], min_val=0, max_val=MAX_EXTRA)
            sp.wait_ge(first.scattered, 16 * E)
            with sp.If(n > 0):
                sp.dma_start(extra_cst[:, :], extra_c).then_inc(extra_in, 16)
            sp.nop()
            with sp.Fori(0, MAX_EXTRA) as j:
                with sp.If(j < n):
                    sp.wait_ge(extra_ready, 1)
                    col = sp.value_load(extra[0:1, bass.ds(j, 1)], min_val=0, max_val=P - 1)
                    sp.wait_ge(more.gathered, (j + 1) * 16)
                    for m in range(CPE):
                        if m >= SPLIT:
                            sp.wait_ge(more.lo_dve, j * CPE + (m - SPLIT + 1))
                        sp.dma_start(raw[m % SPLIT][:, :], wexp[bass.ds(((col // NB) * CPE + m) * P, P), :])\
                          .then_inc(more.raw_in[m % SPLIT], 16)
                sp.nop()
            sp.wait_ge(experts_done, 1)
            sp.dma_start(x_end[:, :, :], x1_dram.rearrange("(a p) n -> p a n", p=P)).then_inc(x_end_in, 16)
            y_by_tile = y_dram.rearrange("(k a p) n -> a p k n", k=TOPK, p=P)
            for t in range(TT):
                if t >= 2:
                    sp.wait_ge(end_sum, t - 1)
                sp.dma_start(y_rows[t % 2][:, :, :], y_by_tile[t]).then_inc(y_in[t % 2], 16)
            for t in range(TT):
                sp.wait_ge(end_ready, t + 1)
                sp.dma_start(out[t * P:(t + 1) * P, :], ln_t[t % 2][:, :]).then_inc(out_done[t % 2], 16)
            for i in range(2):
                sp.wait_ge(out_done[i], 16 * TT // 2)

        @block.tensor
        def _(pe):
            def split3(dst, lh, ll, rh, rl, start, stop):
                pe.matmul(dst, lh, rh, start=start, stop=False)
                pe.matmul(dst, lh, rl, start=False, stop=False)
                return pe.matmul(dst, ll, rh, start=False, stop=stop)

            def transpose(dst, src):
                return pe.matmul(dst, src, ident, is_transpose=True, start=True, stop=True)

            def weights(c):
                pe.wait_ge(m_hi, c + 1)
                pe.wait_ge(m_lo, c + 1)

            def columns(mt, ks=range(KT)):
                c, j = chunk_of(mt)
                if ks[0] == 0:
                    weights(c)
                    if mt >= 4:
                        pe.wait_ge(proj_read, mt - 3)
                for k in ks:
                    if mt == SMALL:
                        pe.wait_ge(x_lo, k // 4 + 1)
                    o = (j * KT + k) * P
                    last = split3(bank[mt % 4][:, :], w_hi[c % 2][:, o:o + P], w_lo[c % 2][:, o:o + P],
                                  xT_hi[:, k, :], xT_lo[:, k, :], k == 0, k == KT - 1)
                if ks[-1] == KT - 1:
                    last.then_inc(used if j == 1 or mt == SMALL else first_tile, 1)

            def tokens(n):
                weights(6 + n)
                for t in range(TT):
                    mt = TOK + (n // 2) * TT + t
                    if n % 2 == 0:
                        pe.wait_ge(proj_read, mt - 3)
                    for k in range(4):
                        kk = (n % 2) * 4 + k
                        last = split3(bank[mt % 4][:, :], xT_hi[:, kk, t * P:(t + 1) * P], xT_lo[:, kk, t * P:(t + 1) * P],
                                      w_hi[n % 2][:, k * 512:(k + 1) * 512], w_lo[n % 2][:, k * 512:(k + 1) * 512],
                                      kk == 0, kk == KT - 1)
                last.then_inc(used, 1)

            def level(n):
                pe.wait_ge(qk_ready, min(n, 6) + 1)
                if n >= 1:
                    pe.wait_ge(level_read, n)
                q, k = (q_dec[n % 2], k_dec[n % 2]) if n < 7 else (g_q, g_k)
                for h in range(HEADS):
                    for t in range(TT):
                        last = pe.matmul(bank[4 + h][:, t * P:(t + 1) * P], k[DK * h:DK * h + DK, t * P:(t + 1) * P],
                                         q[DK * h:DK * h + DK, t * P:(t + 1) * P], start=True, stop=True)
                last.then_inc(level_done, 1)

            def carry(n):
                if n == 0:
                    pe.wait_ge(carry_dve, 1)
                    pe.wait_ge(level_read, 8)
                    for t in range(TT):
                        last = transpose(bank[5][:, t * P:(t + 1) * P], k_end[:, t * P:(t + 1) * P])
                elif n == 1:
                    pe.wait_ge(carry_act, 1)
                    pe.wait_ge(proj_read, TOK + TT)
                    for t in range(3):
                        last = pe.matmul(bank[6 + t // 2][:, (t % 2) * 256:(t % 2) * 256 + 256],
                                         k_endT[:, t * P:(t + 1) * P], values[:, t, 256:512], start=True, stop=True)
                elif n == 2:
                    pe.wait_ge(carry_dve, 2)
                    for t in range(TT):
                        o = bank[4 + t // 2][:, (t % 2) * 256:(t % 2) * 256 + 256]
                        if t > 0:
                            pe.matmul(o, q_dec[1][:, t * P:(t + 1) * P], state[:, t - 1, :], start=True, stop=True)
                        for h in range(HEADS):
                            last = pe.matmul(o[:, DH * h:DH * h + DH], scoreT[:, h, t * P:(t + 1) * P],
                                             values[:, t, 256 + DH * h:256 + DH * h + DH], start=t == 0, stop=True,
                                             skip_group_check=True)
                else:
                    pe.wait_ge(carry_dve, 4)
                    for i in range(2):
                        for t in range(TT):
                            last = transpose(bank[6 + i][:, t * P:(t + 1) * P], y_gla[:, t, i * P:(i + 1) * P])
                last.then_inc(carry_pe, 1)

            pe.wait_ge(cst_in, 32)
            for kind, n in EARLY:
                if kind == "mt":
                    columns(n)
                elif kind == "tok":
                    tokens(n)
                elif kind == "level":
                    level(n)
                elif kind == "carry":
                    carry(n)
                else:
                    pe.wait_ge(gla_in, 96)
                    pe.wait_ge(proj_read, 1)
                    pe.matmul(bank[4][:, :], a_up_sb[:, :], ga_sb[:, :], start=True, stop=True).then_inc(decay_pre, 1)

            pe.wait_ge(crow_in, 16 * HEADS)
            pe.wait_ge(pool_ready, 2)
            pe.wait_ge(yT_lo_ready, 2)
            pe.wait_ge(proj_read, TOK + 2 * TT)
            for s in range(FILL_STEPS):
                if s < UNITS:
                    branch, h, qt = unit(s)
                    if s >= 2:
                        pe.wait_ge(exp_done, s - 1)
                    n = (qt + 1) * P
                    a = h % 2 * DH
                    q, k = (f_q[0:DH + 1, h, :], f_k[0:DH + 1, h, :]) if branch == 0 else (
                        m_q[a:a + DH, h // 2, :], m_k[a:a + DH, h // 2, :])
                    pe.matmul(bank[4 + s % 2][:, 0:n], q[:, qt * P:(qt + 1) * P], k[:, 0:n], start=True, stop=True)
                    pe.matmul(bank[4 + s % 2][:, qt * P:n], ident_b, causal, start=False, stop=True,
                              skip_group_check=True).then_inc(score_done, 1)
                if 1 <= s <= UNITS:
                    u = s - 1
                    pe.wait_ge(norm_done, u + 1)
                    pe.wait_ge(pT_read, u)
                    for kt in range(unit(u)[2] + 1):
                        last = transpose(bank[6][:, kt * P:(kt + 1) * P], probs[u % 2][:, kt * P:(kt + 1) * P])
                    last.then_inc(pT_done, 1)
                if fill(s):
                    g, third = fill(s)
                    columns(GATE + g, (range(0, 3), range(3, 6), range(6, 8))[third])
                if 2 <= s < UNITS + 2:
                    u = s - 2
                    branch, h, qt = unit(u)
                    pe.wait_ge(pT_read, u + 1)
                    if u % 8 == 0 and u:
                        pe.wait_ge(yT_lo_ready, 2 + u // 8)
                    col = 512 * branch + DH * h
                    a = h % 2 * DH
                    for kt in range(qt + 1):
                        last = pe.matmul(bank[7][a:a + DH, qt * P:(qt + 1) * P], values[:, kt, col:col + DH],
                                         probsT[u % 2][:, kt * P:(kt + 1) * P], start=kt == 0, stop=kt == qt)
                    last.then_inc(pv_done, 1)

            for kind, n in LATE:
                if kind == "gate":
                    columns(GATE + n)
                    continue
                c = W_UP[n]
                weights(c)
                if n == 0:
                    pe.wait_ge(yT_lo_ready, 6)
                for b in range(3):
                    i = 3 * n + b
                    if i >= 4:
                        pe.wait_ge(up_read, i - 3)
                    for ct in range(2):
                        o = ((n % 2 * 3 + b) * 2 + ct) * P
                        y = (0, 2, 4)[b] + ct
                        last = split3(bank[4 + i % 4][:, :], w_hi[c % 2][:, o:o + P], w_lo[c % 2][:, o:o + P],
                                      yT_hi[:, y, :], yT_lo[:, y, :], ct == 0, ct == 1)
                    last.then_inc(up_signal(i)[0], 1)
            for n in range(4):
                weights(W_OUT + n)
                if n == 0:
                    pe.wait_ge(proj_read, GATE + 24)
                if n == 2:
                    pe.wait_ge(up_read, 3 * KT)
                for t in range(TT):
                    for k in range(4):
                        kk = n % 2 * 4 + k
                        pe.wait_ge(merged_lo_ready, kk + 1)
                        last = split3(bank[n // 2 * 4 + t][:, :],
                                      merged_hi[:, kk, t * P:(t + 1) * P], merged_lo[:, kk, t * P:(t + 1) * P],
                                      w_hi[n % 2][:, k * 512:(k + 1) * 512], w_lo[n % 2][:, k * 512:(k + 1) * 512],
                                      kk == 0, kk == KT - 1)
                last.then_inc(used, 1)

            def x1_transposes(t):
                pe.wait_ge(x1_ready, t + 1)
                for h in range(2):
                    n = 2 * t + h
                    if n >= 4:
                        pe.wait_ge(x1T_read, n - 3)
                    for k in range(4):
                        last = transpose(bank[n % 4][:, k * P:(k + 1) * P], x1[:, t, (4 * h + k) * P:(4 * h + k + 1) * P])
                    last.then_inc(x1T_done, 1)

            def router(t):
                pe.wait_ge(x1T_read, 2 * t + 2)
                for k in range(KT):
                    last = pe.matmul(bank[4][:, t * E:(t + 1) * E], x1T[:, k, t * P:(t + 1) * P], w_r[:, k, :],
                                     start=k == 0, stop=k == KT - 1)
                return last

            pe.wait_ge(w_r_in, 16)
            x1_transposes(0)
            x1_transposes(1)
            router(0)
            for t in range(2, TT):
                x1_transposes(t)
                router(t - 1)
            router(TT - 1).then_inc(logit_done, 1)
            pe.wait_ge(hits_ready, 1)
            for t in range(TT):
                for a in range(t + 1):
                    last = pe.matmul(bank[5][:, t * E:(t + 1) * E], before if a == t else ones_b, hits[:, a, :],
                                     start=a == 0, stop=a == t)
            last.then_inc(pos_done, 1)
            for a in range(TT):
                last = pe.matmul(bank[7][:, 0:E], ones_b, hits[:, a, :], start=a == 0, stop=a == TT - 1)
            last.then_inc(counted, 1)
            for n in range(TT * TOPK):
                pe.wait_ge(onehot_ready, n + 1)
                last = pe.matmul(bank[6][:, 0:P], onehot_s[:, n, :], onehot_c[:, n, :], start=n == 0, stop=n == TT * TOPK - 1)
            last.then_inc(onehot_used, 1)

            def transposes4(w, dst, src, o):
                for k in range(4):
                    last = transpose(dst[:, k * P:(k + 1) * P], src[:, o + k * P:o + (k + 1) * P])
                last.then_inc(w.tr, 1)

            def expert(w, e, expert_no, last_one):
                w_ready = lambda m: (pe.wait_ge(w.hi, e * CPE + (m + 1)), w.wait_lo(pe, e, m))
                n_a, n_b = w.transposes(e, last_one)
                if w.alone:
                    pe.wait_ge(w.gathered, (e + 1) * 16)
                    for h in range(2):
                        transposes4(w, bank[6 + h], x_rows, 512 * h)
                pe.wait_ge(w.tr_hi, e * 4 + 2)
                pe.wait_ge(w.tr_lo, e * 4 + 2)
                for half in range(2):
                    banks = (bank[2 * half], bank[2 * half + 1])
                    if not w.alone and not (isinstance(e, int) and e == 0):
                        pe.wait_ge(w.glu_read, e * 2 + (half - 1))
                    for kp in range(4):
                        m = 4 * half + kp
                        w_ready(m)
                        if kp == 3:
                            for b in range(2):
                                o = (2 * half + b) * 512
                                pe.matmul(banks[b][:, :], pick[:, bass.ds(expert_no, 1)].to_broadcast([96, P]),
                                          bias3[:, o:o + 512], start=False, stop=False)
                        for k2 in range(2):
                            k = 2 * kp + k2
                            cols = [slice(k2 * D + 512 * b, k2 * D + 512 * b + 512) for b in range(2)]
                            for b in range(2):
                                pe.matmul(banks[b][:, :], xe_hi[:, k, :], w_hi[m % 4][:, cols[b]], start=k == 0, stop=False)
                                pe.matmul(banks[b][:, :], xe_hi[:, k, :], w_lo[m % 4][:, cols[b]], start=False, stop=False)
                            for b in range(2):
                                last = pe.matmul(banks[b][:, :], xe_lo[:, k, :], w_hi[m % 4][:, cols[b]], start=False,
                                                 stop=k == KT - 1)
                        last.then_inc(w.used, 1)
                pipelined = not w.alone and not last_one
                pe.wait_ge(w.act_ready, e * 2 + 1)
                pe.wait_ge(w.tr_lo, n_a - 1)
                transposes4(w, bank[6], act[0], 0)
                if pipelined:
                    pe.wait_ge(w.gathered, (e + 2) * 16)
                    pe.wait_ge(w.tr_lo, n_a)
                    transposes4(w, bank[7], x_rows, 0)
                if not w.alone and not (isinstance(e, int) and e == 0):
                    pe.wait_ge(w.y_copied, e)
                for q in range(4):
                    m = 8 + q
                    if q == 0:
                        pe.wait_ge(w.tr_lo, n_a + 1)
                    if q == 1:
                        pe.wait_ge(w.act_ready, e * 2 + 2)
                        pe.wait_ge(w.tr_lo, n_b - 1)
                        transposes4(w, bank[6] if pipelined else bank[7], act[1], 0)
                    if q == 2:
                        if pipelined:
                            pe.wait_ge(w.tr_lo, n_b)
                            transposes4(w, bank[7], x_rows, 512)
                        pe.wait_ge(w.tr_lo, n_b + 1)
                    w_ready(m)
                    if q == 3:
                        for b in range(2):
                            o = 2 * D + 512 * b
                            pe.matmul(bank[4 + b][:, :], pick[:, bass.ds(expert_no, 1)].to_broadcast([96, P]),
                                      bias3[:, o:o + 512], start=False, stop=False)
                    for k2 in range(2):
                        k = 2 * q + k2
                        ah, al = aT_hi[k // 4][:, k % 4, :], aT_lo[k // 4][:, k % 4, :]
                        cols = [slice(k2 * D + 512 * b, k2 * D + 512 * b + 512) for b in range(2)]
                        for b in range(2):
                            pe.matmul(bank[4 + b][:, :], ah, w_hi[m % 4][:, cols[b]], start=k == 0, stop=False)
                            pe.matmul(bank[4 + b][:, :], ah, w_lo[m % 4][:, cols[b]], start=False, stop=False)
                        for b in range(2):
                            last = pe.matmul(bank[4 + b][:, :], al, w_hi[m % 4][:, cols[b]], start=False, stop=k == KT - 1)
                    last.then_inc(w.used, 1)

            pe.wait_ge(route_ready, 2)
            pe.wait_ge(bias_ready, 1)
            pe.wait_ge(first.gathered, 16)
            for h in range(2):
                transposes4(first, bank[6 + h], x_rows, 512 * h)
            passes(pe, lambda e, p, last_one: expert(first, e, e, last_one))
            n = pe.value_load(n_extra[0:1, 0:1], min_val=0, max_val=MAX_EXTRA)
            with pe.Fori(0, MAX_EXTRA) as j:
                with pe.If(j < n):
                    pe.wait_ge(extra_ready, 1)
                    col = pe.value_load(extra[0:1, bass.ds(j, 1)], min_val=0, max_val=P - 1)
                    expert(more, j, col // NB, False)
                pe.nop()

        @block.scalar
        def _(act_e):
            link = linked(act_e, act_step)
            A = act_e.activation

            def high(c):
                act_e.wait_ge(mix_in[c % RAW_MIX], 16 * (c // RAW_MIX + 1))
                if c >= 2:
                    act_e.wait_ge(used, c - 1)
                A(w_hi[c % 2][:, :], raw[c % RAW_MIX][:, :], ACT.Copy).then_inc(m_hi, 1)

            def after(kind, n):
                c = freed(kind, n)
                if c is not None and c + 2 < N_MIX:
                    high(c + 2)

            def copy_out(mt):
                act_e.wait_ge(*tile_done(mt))
                if mt == TOK:
                    act_e.wait_ge(pool_ready, 1)
                b = bank[mt % 4]
                if mt == SMALL:
                    A(ga_sb[:, :], b[0:16, :], ACT.Copy)
                    ins = A(f_raw[:, :], b[32:32 + HEADS, :], ACT.Copy)
                elif mt == GQ:
                    ins = A(g_q[:, :], b[:, :], ACT.Copy, scale=DK ** -0.5)
                elif mt == GK:
                    ins = A(g_k[:, :], b[:, :], ACT.Copy)
                elif mt < MQ:
                    q = mt < FK
                    h = 2 * (mt - (FQ if q else FK))
                    for i in range(2):
                        ins = A((f_q if q else f_k)[0:DH, h + i, :], b[DH * i:DH * i + DH, :], ACT.Copy,
                                scale=DH ** -0.5 if q else 1.0)
                elif mt < MK:
                    ins = A(m_q[:, mt - MQ, :], b[:, :], ACT.Copy, scale=DH ** -0.5)
                elif mt < TOK:
                    ins = A(m_k[:, mt - MK, :], b[:, :], ACT.Copy)
                elif mt < TOK + TT:
                    ins = A(values[:, mt - TOK, 0:512], b[:, :], ACT.Copy)
                elif mt < GATE:
                    t = mt - TOK - TT
                    A(values[:, t, 512:768], b[:, 0:256], ACT.Copy)
                    ins = A(values[:, t, 768:1024], b[:, 256:512], ACT.Silu)
                else:
                    g = mt - GATE
                    if g >= GATE_SLOTS:
                        act_e.wait_ge(up_read, g - GATE_SLOTS + 1)
                    ins = A(gates[:, g % GATE_SLOTS, :], b[:, :], ACT.Copy if g < GATE_SLOTS else ACT.Sigmoid)
                ins.then_inc(proj_read, 1)

            def ratio_exp(n):
                act_e.wait_ge(diff_ready, n + 1)
                link(A(ratio[:, :], ratio[:, :], ACT.Abs))
                A(ratio[:, :], ratio[:, :], ACT.Exp, scale=-1.0 / TAU).then_inc(ratio_ready, 1)

            for h in range(2):
                act_e.wait_ge(x_in[h], 16)
                A(xT_hi[:, 4 * h:4 * h + 4, :], xT_in[:, 4 * h:4 * h + 4, :], ACT.Copy).then_inc(x_hi, 1)
                high(h)
            for kind, n in EARLY:
                if kind == "mt":
                    copy_out(n)
                elif kind == "tok" and n % 2:
                    for t in range(TT):
                        copy_out(TOK + n // 2 * TT + t)
                elif kind == "decay":
                    act_e.wait_ge(decay_pre, 1)
                    link(A(log1p[:, :], bank[4][:, :], ACT.Abs, bias=a_b_sb[:, 0:1]))
                    link(A(f_log[:, :], f_raw[:, :], ACT.Abs, bias=fb_sb[:, 0:1]))
                    link(A(log1p[:, :], log1p[:, :], ACT.Exp, scale=-1.0))
                    link(A(f_log[:, :], f_log[:, :], ACT.Exp, scale=-1.0))
                    A(log1p[:, :], log1p[:, :], ACT.Ln, bias=1.0)
                    A(f_log[:, :], f_log[:, :], ACT.Ln, bias=1.0).then_inc(log_ready, 1)
                    ratio_exp(0)
                    ratio_exp(1)
                elif kind == "level":
                    if n + 2 < 7:
                        ratio_exp(n + 2)
                    if n == 5:
                        act_e.wait_ge(level_read, 6)
                        act_e.wait_ge(qk_ready, 7)
                        A(end_dec[:, :], decay[:, P - 1::P], ACT.Exp, scale=-1.0 / TAU)
                        A(ratio[:, :], decay[:, :], ACT.Exp, scale=-1.0 / TAU).then_inc(ratio_ready, 1)
                    if n == 6:
                        act_e.wait_ge(diff_ready, 8)
                        A(k_end[:, :], k_end[:, :], ACT.Exp, scale=1.0 / TAU).then_inc(ratio_ready, 1)
                elif kind == "carry" and n == 0:
                    act_e.wait_ge(carry_pe, 1)
                    A(k_endT[:, :], bank[5][:, :], ACT.Copy).then_inc(carry_act, 1)
                elif kind == "carry" and n == 2:
                    act_e.wait_ge(carry_pe, 3)
                    for i in range(2):
                        A(squares[:, 512 * i:512 * i + 512], bank[4 + i][:, :], ACT.Square).then_inc(carry_act, 1)
                    act_e.wait_ge(carry_dve, 3)
                    A(rms[:, :], rms[:, :], ACT.Sqrt).then_inc(carry_act, 1)
                elif kind == "carry" and n == 3:
                    act_e.wait_ge(carry_pe, 4)
                    for i in range(2):
                        A(yT_hi[:, 2 + i, :], bank[6 + i][:, :], ACT.Copy).then_inc(yT_hi_ready, 1)
                after(kind, n)

            for s in range(FILL_STEPS + 1):
                if s >= 3 and s % 3 == 0:
                    g = s // 3 - 1
                    copy_out(GATE + g)
                    after("gate", g)
                if s < UNITS:
                    act_e.wait_ge(max_ready, s + 1)
                    if s >= 2:
                        act_e.wait_ge(pT_done, s - 1)
                    n = (unit(s)[2] + 1) * P
                    A(probs[s % 2][:, 0:n], bank[4 + s % 2][:, 0:n], ACT.Exp, bias=row_max[:, s % 2:s % 2 + 1],
                      accum_out=row_sum[:, s % 2:s % 2 + 1]).then_inc(exp_done, 1)
                if 1 <= s <= UNITS:
                    u = s - 1
                    act_e.wait_ge(pT_done, u + 1)
                    if u >= 2:
                        act_e.wait_ge(pv_done, u - 1)
                    n = (unit(u)[2] + 1) * P
                    A(probsT[u % 2][:, 0:n], bank[6][:, 0:n], ACT.Copy).then_inc(pT_read, 1)
                if s >= 10 and (s - 10) % 8 == 0 and (s - 10) // 8 < 3 or s == FILL_STEPS:
                    pair = min((s - 10) // 8, 3)
                    act_e.wait_ge(pv_done, 8 * pair + 8)
                    A(yT_hi[:, (0, 1, 4, 5)[pair], :], bank[7][:, :], ACT.Copy).then_inc(yT_hi_ready, 1)

            act_e.wait_ge(proj_read, GATE + 12)
            for d in range(4):
                A(gates[:, 3 * d:3 * d + 3, :], gates[:, 3 * d:3 * d + 3, :], ACT.Sigmoid).then_inc(gate_sig, 1)
            for kind, n in LATE:
                if kind == "gate":
                    copy_out(GATE + n)
                else:
                    act_e.wait_ge(merged_ready, n + 1)
                    A(merged_hi[:, n, :], mix_acc[n % 2][:, :], ACT.Copy).then_inc(merged_hi_ready, 1)
                after(kind, n)
            for n in range(2):
                after("out", n)
            def expert_high(w, e, p, m):
                w.wait_raw(act_e, e, p, m)
                A(w_hi[m % 4][:, :], w.raw(p, m)[:, :], ACT.Copy).then_inc(w.hi, 1)

            for m in range(2):
                act_e.wait_ge(used, N_MIX - 1 + m)
                expert_high(first, 0, 0, m)
            act_e.wait_ge(var_ready, 1)
            A(std[:, :], std[:, :], ACT.Sqrt).then_inc(std_ready, 1)
            for n in range(2 * TT):
                act_e.wait_ge(x1T_done, n + 1)
                t, h = n // 2, n % 2
                A(x1T[:, 4 * h:4 * h + 4, t * P:(t + 1) * P], bank[n % 4][:, :].rearrange("p (k n) -> p k n", k=4),
                  ACT.Copy).then_inc(x1T_read, 1)
            act_e.wait_ge(top_ready, 1)
            A(exp4[:, :, :], exp4[:, :, :], ACT.Exp).then_inc(gate_exp, 1)
            act_e.wait_ge(x1_out, 16 * TT)
            for m in (2, 3):
                expert_high(first, 0, 0, m)

            def xe_high(w, h, src):
                A(xe_hi[:, 4 * h:4 * h + 4, :], src[:, :].rearrange("p (k n) -> p k n", k=4), ACT.Copy)\
                    .then_inc(w.tr_hi, 1)

            def expert(w, e, p, last_one):
                n_a, n_b = w.transposes(e, last_one)
                pipelined = not w.alone and not last_one
                if w.alone:
                    for m in range(SPLIT):
                        expert_high(w, e, p, m)
                    for h in range(2):
                        act_e.wait_ge(w.tr, e * 4 + (h + 1))
                        xe_high(w, h, bank[6 + h])
                for m in range(CPE):
                    if m == 7:
                        act_e.wait_ge(w.tr, n_a + 1)
                        A(aT_hi[0][:, :, :], bank[6][:, :].rearrange("p (k n) -> p k n", k=4), ACT.Copy).then_inc(w.tr_hi, 1)
                        act_e.wait_ge(w.glu_read, e * 2 + 2)
                        A(glu_s[:, :], glu_g[:, :], ACT.Sigmoid, scale=SWIGLU).then_inc(w.sig, 1)
                        if pipelined:
                            act_e.wait_ge(w.tr, n_a + 2)
                            xe_high(w, 0, bank[7])
                    if m == 8:
                        act_e.wait_ge(w.tr, n_b + 1)
                        A(aT_hi[1][:, :, :], (bank[6] if pipelined else bank[7])[:, :].rearrange("p (k n) -> p k n", k=4),
                          ACT.Copy).then_inc(w.tr_hi, 1)
                    if m == 9 and pipelined:
                        act_e.wait_ge(w.tr, n_b + 2)
                        xe_high(w, 1, bank[7])
                    act_e.wait_ge(w.used, e * CPE + (m + 1))
                    if m == 11:
                        if not w.alone and not (isinstance(e, int) and e == 0):
                            act_e.wait_ge(w.scattered, e * 16)
                        for b in range(2):
                            ins = A(y_sb[:, 512 * b:512 * b + 512], bank[4 + b][:, :], ACT.Copy)
                        ins.then_inc(w.y_copied, 1)
                    if m + LOOK < CPE or pipelined:
                        expert_high(w, e, p, m + LOOK)
                    if m == 3:
                        act_e.wait_ge(w.glu_read, e * 2 + 1)
                        A(glu_s[:, :], glu_g[:, :], ACT.Sigmoid, scale=SWIGLU).then_inc(w.sig, 1)

            for h in range(2):
                act_e.wait_ge(first.tr, h + 1)
                xe_high(first, h, bank[6 + h])
            passes(act_e, lambda e, p, last_one: expert(first, e, p, last_one))
            n = act_e.value_load(n_extra[0:1, 0:1], min_val=0, max_val=MAX_EXTRA)
            with act_e.Fori(0, MAX_EXTRA) as j:
                with act_e.If(j < n):
                    expert(more, j, 0, False)
                act_e.nop()
            for t in range(TT):
                act_e.wait_ge(y_in[t % 2], 16 * (t // 2 + 1))
                if t >= 2:
                    act_e.wait_ge(end_scaled, t - 1)
                A(res[t % 2][:, :], y_rows[t % 2][:, 0, :], ACT.Copy, scale=gate_w[:, t, 0:1]).then_inc(end_first, 1)
                act_e.wait_ge(end_var, t + 1)
                A(std[:, t:t + 1], std[:, t:t + 1], ACT.Sqrt).then_inc(end_std, 1)

        @block.vector
        def _(dve):
            link = linked(dve, dve_step)
            TTO, TS, STT = dve.tensor_tensor, dve.tensor_scalar, dve.scalar_tensor_tensor

            def low(c):
                dve.wait_ge(m_hi, c + 1)
                TTO(w_lo[c % 2][:, :], raw[c % RAW_MIX][:, :], w_hi[c % 2][:, :].bitcast(F32), ALU.subtract).then_inc(m_lo, 1)

            def after(kind, n):
                c = freed(kind, n)
                if c is not None and c + 2 < N_MIX:
                    low(c + 2)

            def blocks(x, size):
                return x[:, :].rearrange("p (n s) -> p n s", s=size)

            def difference(n):
                s = 2 * LEVELS[n]
                if n >= 1:
                    dve.wait_ge(qk_ready, n)
                ref = blocks(decay, s)[:, :, LEVELS[n] - 1:LEVELS[n]].to_broadcast([P, T // s, s])
                TTO(blocks(ratio, s), blocks(decay, s), ref, ALU.subtract).then_inc(diff_ready, 1)

            def scale_qk(n):
                dve.wait_ge(ratio_ready, n + 1)
                if n >= 2:
                    dve.wait_ge(level_done, n - 1)
                TTO(q_dec[n % 2][:, :], g_q[:, :], ratio[:, :], ALU.mult)
                TTO(k_dec[n % 2][:, :], g_k[:, :], ratio[:, :], ALU.mult).then_inc(qk_ready, 1)

            for h in range(2):
                dve.wait_ge(x_hi, h + 1)
                TTO(xT_lo[:, 4 * h:4 * h + 4, :], xT_in[:, 4 * h:4 * h + 4, :], xT_hi[:, 4 * h:4 * h + 4, :].bitcast(F32),
                    ALU.subtract).then_inc(x_lo, 1)
                low(h)
            for kind, n in EARLY:
                if kind == "decay":
                    dve.wait_ge(log_ready, 1)
                    dve.wait_ge(cst_in, 32)
                    link(TS(ratio[:, :], bank[4][:, :], a_b_sb[:, 0:1], 0.0, ALU.add, ALU.min))
                    link(TS(f_raw[:, :], f_raw[:, :], fb_sb[:, 0:1], 0.0, ALU.add, ALU.min))
                    link(TTO(ratio[:, :], log1p[:, :], ratio[:, :], ALU.subtract))
                    link(TTO(f_log[:, :], f_log[:, :], f_raw[:, :], ALU.subtract))
                    for t in range(TT):
                        dve.tensor_tensor_scan(decay[:, t * P:(t + 1) * P], ones, ratio[:, t * P:(t + 1) * P], 0.0,
                                               ALU.mult, ALU.add)
                        link(dve.tensor_tensor_scan(f_cum[:, t * P:(t + 1) * P], ones[0:HEADS, :], f_log[:, t * P:(t + 1) * P],
                                                    f_cum[:, t * P - 1:t * P] if t else 0.0, ALU.mult, ALU.add))
                    dve.tensor_copy(f_raw[:, :], f_cum[:, :]).then_inc(crow_ready, 1)
                    dve.wait_ge(proj_read, 3)
                    for m in range(2):
                        difference(m)
                        scale_qk(m)
                elif kind == "level":
                    dve.wait_ge(level_done, n + 1)
                    if n == 0:
                        dve.wait_ge(gla_in, 96)
                        dve.wait_ge(pool_ready, 1)
                    mask = level_mask[:, n, :].unsqueeze(1).to_broadcast([P, TT, P])
                    for h in range(HEADS):
                        ins = dve.copy_predicated(scoreT[:, h, :].rearrange("p (t s) -> p t s", t=TT), mask,
                                                  bank[4 + h][:, :].rearrange("p (t s) -> p t s", t=TT))
                    ins.then_inc(level_read, 1)
                    if n + 2 < 7:
                        difference(n + 2)
                        scale_qk(n + 2)
                    if n == 4:
                        b = blocks(decay, P)
                        TTO(blocks(k_end, P), b, b[:, :, P - 1:P].to_broadcast([P, TT, P]), ALU.subtract).then_inc(diff_ready, 1)
                    if n == 6:
                        dve.wait_ge(ratio_ready, 8)
                        TTO(q_dec[1][:, :], g_q[:, :], ratio[:, :], ALU.mult)
                        dve.wait_ge(ratio_ready, 9)
                        TTO(k_end[:, :], g_k[:, :], k_end[:, :], ALU.mult).then_inc(carry_dve, 1)
                elif kind == "carry" and n == 1:
                    dve.wait_ge(carry_pe, 2)
                    for t in range(3):
                        link(TTO(state[:, t, :], bank[6 + t // 2][:, (t % 2) * 256:(t % 2) * 256 + 256], head_mask[:, :], ALU.mult))
                    link(STT(state[:, 1, :], state[:, 0, :], end_dec[:, 1:2], state[:, 1, :], ALU.mult, ALU.add))
                    STT(state[:, 2, :], state[:, 1, :], end_dec[:, 2:3], state[:, 2, :], ALU.mult, ALU.add).then_inc(carry_dve, 1)
                elif kind == "carry" and n == 2:
                    dve.wait_ge(proj_read, TOK + 2 * TT)
                    gb = norm_gb[:, :].unsqueeze(1).to_broadcast([P, TT, 256])
                    link(TTO(values[:, :, 768:1024], values[:, :, 768:1024], gb, ALU.mult))
                    dve.wait_ge(carry_act, 3)
                    link(dve.tensor_reduce(rms[:, :], squares[:, :].rearrange("p (g d) -> p g d", d=DH), AX.X, ALU.add))
                    TS(rms[:, :], rms[:, :], 1.0 / DH, RMS_EPS, ALU.mult, ALU.add).then_inc(carry_dve, 1)
                    dve.wait_ge(carry_act, 4)
                    dve.wait_ge(crow_in, 16 * HEADS)
                    link(dve.reciprocal(rms[:, :], rms[:, :]))
                    for i in range(2):
                        yv = y_gla[:, 2 * i:2 * i + 2, :].rearrange("p t (h d) -> p (t h) d", d=DH)
                        link(TTO(yv, bank[4 + i][:, :].rearrange("p (g d) -> p g d", d=DH),
                                 rms[:, 8 * i:8 * i + 8].unsqueeze(2).to_broadcast([P, 8, DH]), ALU.mult))
                    TTO(y_gla[:, :, :], y_gla[:, :, :], values[:, :, 768:1024], ALU.mult).then_inc(carry_dve, 1)
                elif kind == "carry" and n == 3:
                    for i in range(2):
                        dve.wait_ge(yT_hi_ready, i + 1)
                        TTO(yT_lo[:, 2 + i, :], bank[6 + i][:, :], yT_hi[:, 2 + i, :].bitcast(F32), ALU.subtract)\
                            .then_inc(yT_lo_ready, 1)
                after(kind, n)

            for s in range(FILL_STEPS + 1):
                if s >= 3 and s % 3 == 0:
                    after("gate", s // 3 - 1)
                if s < UNITS:
                    dve.wait_ge(score_done, s + 1)
                    n = (unit(s)[2] + 1) * P
                    m = slice(s % 2, s % 2 + 1)
                    dve.tensor_reduce(row_max[:, m], bank[4 + s % 2][:, 0:n], AX.X, ALU.max, negate=True).then_inc(max_ready, 1)
                    dve.wait_ge(exp_done, s + 1)
                    link(dve.reciprocal(row_inv[:, m], row_sum[:, m]))
                    TS(probs[s % 2][:, 0:n], probs[s % 2][:, 0:n], row_inv[:, m], None, ALU.mult).then_inc(norm_done, 1)
                if s >= 10 and (s - 10) % 8 == 0 and (s - 10) // 8 < 3 or s == FILL_STEPS:
                    pair = min((s - 10) // 8, 3)
                    dve.wait_ge(yT_hi_ready, 3 + pair)
                    y = (0, 1, 4, 5)[pair]
                    TTO(yT_lo[:, y, :], bank[7][:, :], yT_hi[:, y, :].bitcast(F32), ALU.subtract).then_inc(yT_lo_ready, 1)

            for kind, n in LATE:
                if kind == "up":
                    if n < 4:
                        dve.wait_ge(gate_sig, n + 1)
                    else:
                        dve.wait_ge(proj_read, GATE + 3 * n + 3)
                    if n >= 2:
                        dve.wait_ge(merged_hi_ready, n - 1)
                    acc, tmp = mix_acc[n % 2], mix_tmp
                    for b in range(3):
                        i = 3 * n + b
                        dve.wait_ge(*up_signal(i))
                        to = acc if b == 0 else tmp[b - 1]
                        TTO(to[:, :], bank[4 + i % 4][:, :], gates[:, i % GATE_SLOTS, :], ALU.mult).then_inc(up_read, 1)
                    dve.wait_ge(up_read, 3 * n + 3)
                    link(TTO(acc[:, :], acc[:, :], tmp[0][:, :], ALU.add))
                    TTO(acc[:, :], acc[:, :], tmp[1][:, :], ALU.add).then_inc(merged_ready, 1)
                    dve.wait_ge(merged_hi_ready, n + 1)
                    TTO(merged_lo[:, n, :], acc[:, :], merged_hi[:, n, :].bitcast(F32), ALU.subtract).then_inc(merged_lo_ready, 1)
                after(kind, n)
                if (kind, n) == ("up", 3):
                    dve.wait_ge(bias_in, 48)
                    link(dve.tensor_copy(bias3[:, :], bias_f[:, :]))
                    link(TTO(bias_f[:, :], bias_f[:, :], bias3[:, :], ALU.subtract))
                    dve.tensor_copy(bias3[32:64, :], bias_f[32:64, :])
                    link(dve.tensor_copy(bias3[64:96, :], bias_f[64:96, :]))
                    link(TTO(bias_f[64:96, :], bias_f[64:96, :], bias3[64:96, :], ALU.subtract))
                    dve.tensor_copy(bias3[64:96, :], bias_f[64:96, :]).then_inc(bias_ready, 1)
            for n in range(2):
                after("out", n)

            dve.wait_ge(tok_in, 64)
            for half in range(2):
                dve.wait_ge(used, 28 + 2 * half)
                for t in range(TT):
                    cols = slice(512 * half, 512 * half + 512)
                    link(STT(x1[:, t, cols], x_tok[:, t, cols], ALPHA, bank[4 * half + t][:, :], ALU.mult, ALU.add))
                    link(dve.bn_stats(stats[:, t, 6 * half:6 * half + 6], x1[:, t, cols]))
            for t in range(TT):
                link(dve.bn_aggr(mean_var[:, t, :], stats[:, t, :]))
            TS(std[:, :], mean_var[:, :, 1], LN_EPS, None, ALU.add).then_inc(var_ready, 1)
            dve.wait_ge(std_ready, 1)
            link(dve.reciprocal(std[:, :], std[:, :]))
            for t in range(TT):
                link(TS(x1[:, t, :], x1[:, t, :], mean_var[:, t, 0:1], std[:, t:t + 1], ALU.subtract, ALU.mult))
                TTO(x1[:, t, :], x1[:, t, :], ln_g[:, :], ALU.mult).then_inc(scaled, 1)

            def expert_low(w, e, p, m):
                dve.wait_ge(w.hi, e * CPE + (m + 1))
                TTO(w_lo[m % 4][:, :], w.raw(p, m)[:, :], w_hi[m % 4][:, :].bitcast(F32), ALU.subtract).then_inc(w.lo_dve, 1)

            for m in range(2):
                expert_low(first, 0, 0, m)
            dve.wait_ge(logit_done, 1)
            link(TTO(logits[:, :, :], bank[4][:, 0:TT * E].rearrange("p (t e) -> p t e", t=TT),
                     b_r[:, :].unsqueeze(1).to_broadcast([P, TT, E]), ALU.add))
            for t in range(TT):
                link(dve.max(top_v[:, t, :], logits[:, t, :]))
            TTO(exp4[:, :, :], top_v[:, :, 0:TOPK], top_v[:, :, 0:1].to_broadcast([P, TT, TOPK]), ALU.subtract)\
                .then_inc(top_ready, 1)
            for t in range(TT):
                link(dve.max_index(top_i[:, t, :], top_v[:, t, :], logits[:, t, :]))
            link(dve.tensor_copy(ix_f[:, :, :], top_i[:, :, 0:TOPK]))
            link(TTO(chosen[:, :, :, :], iota[:, 0:E].unsqueeze(1).unsqueeze(1).to_broadcast([P, TT, TOPK, E]),
                     ix_f[:, :, :].unsqueeze(3).to_broadcast([P, TT, TOPK, E]), ALU.is_equal))
            with nc.allow_low_precision(reason="sums of zeros and at most one one"):
                dve.tensor_reduce(hits[:, :, :], chosen[:, :, :, :].rearrange("p t k e -> p t e k"), AX.X, ALU.add)\
                   .then_inc(hits_ready, 1)
            dve.wait_ge(gate_exp, 1)
            link(dve.tensor_reduce(exp_sum[:, :], exp4[:, :, :], AX.X, ALU.add))
            link(dve.reciprocal(exp_sum[:, :], exp_sum[:, :]))
            link(TTO(gate_w[:, :, :], exp4[:, :, :], exp_sum[:, :].unsqueeze(2).to_broadcast([P, TT, TOPK]), ALU.mult))
            dve.wait_ge(pos_done, 1)
            link(TTO(places_of[:, :, :, :], chosen[:, :, :, :],
                     bank[5][:, 0:TT * E].rearrange("p (t e) -> p t e", t=TT).unsqueeze(2).to_broadcast([P, TT, TOPK, E]),
                     ALU.mult))
            link(dve.tensor_reduce(pos[:, :], places_of[:, :, :, :].rearrange("p t k e -> p (t k) e"), AX.X, ALU.add))
            link(TS(blk[:, :], pos[:, :], float(P), None, ALU.is_ge))
            for b in (2, 3):
                link(STT(blk[:, :], pos[:, :], float(b * P), blk[:, :], ALU.is_ge, ALU.add))
            link(STT(slot[:, :], blk[:, :], -float(P), pos[:, :], ALU.mult, ALU.add))
            link(STT(col_f[:, :], ix_f[:, :, :].rearrange("p t k -> p (t k)"), float(NB), blk[:, :], ALU.mult, ALU.add))
            for n in range(TT * TOPK):
                t, k = n // TOPK, n % TOPK
                TS(onehot_s[:, n, :], iota, slot[:, n:n + 1], None, ALU.is_equal)
                TS(onehot_c[:, n, :], iota, col_f[:, n:n + 1], row_id[:, k * TT + t:k * TT + t + 1], ALU.is_equal, ALU.mult)\
                    .then_inc(onehot_ready, 1)
            dve.wait_ge(onehot_used, 1)
            link(TS(table[:, :], bank[6][:, 0:P], -1.0, None, ALU.add))
            dve.tensor_copy(scatter_ix[:, :], table[:, :])
            link(TS(wrap[:, :], table[:, :], float(T), None, ALU.is_ge))
            for k in (2, 3):
                link(STT(wrap[:, :], table[:, :], float(k * T), wrap[:, :], ALU.is_ge, ALU.add))
            link(STT(wrapped[:, :], wrap[:, :], -float(T), table[:, :], ALU.mult, ALU.add))
            dve.tensor_copy(gather_ix[:, :], wrapped[:, :]).then_inc(route_ready, 1)
            dve.wait_ge(counted, 1)
            link(dve.tensor_copy(counts[:, :], bank[7][0:1, 0:E]))
            link(TS(over[:, :], counts[:, :], float(P), None, ALU.is_gt))
            for k in (2, 3):
                link(STT(over[:, :], counts[:, :], float(k * P), over[:, :], ALU.is_gt, ALU.add))
            link(dve.tensor_reduce(junk[0:1, 0:1], over[:, :], AX.X, ALU.add))
            dve.tensor_copy(n_extra[:, :], junk[0:1, 0:1]).then_inc(route_ready, 1)
            for m in (2, 3):
                expert_low(first, 0, 0, m)

            def xe_low(w, h, src):
                TTO(xe_lo[:, 4 * h:4 * h + 4, :], src[:, :].rearrange("p (k n) -> p k n", k=4),
                    xe_hi[:, 4 * h:4 * h + 4, :].bitcast(F32), ALU.subtract).then_inc(w.tr_lo, 1)

            def act_low(w, h, src):
                TTO(aT_lo[h][:, :, :], src[:, :].rearrange("p (k n) -> p k n", k=4), aT_hi[h][:, :, :].bitcast(F32),
                    ALU.subtract).then_inc(w.tr_lo, 1)

            def clamp(w, e, half):
                dve.wait_ge(w.used, e * CPE + (4 * half + 4))
                TS(glu_g[:, :], bank[2 * half][:, :], LIMIT, None, ALU.min)
                TS(glu_u[:, :], bank[2 * half + 1][:, :], LIMIT, -LIMIT, ALU.min, ALU.max).then_inc(w.glu_read, 1)

            def activate(w, e, half):
                dve.wait_ge(w.sig, e * 2 + (half + 1))
                TTO(glu_g[:, :], glu_g[:, :], glu_s[:, :], ALU.mult).then_inc(w.gated, 1)
                dve.wait_ge(w.gated, e * 2 + (half + 1))
                STT(act[half][:, :], glu_u[:, :], 1.0, glu_g[:, :], ALU.add, ALU.mult).then_inc(w.act_ready, 1)

            def expert(w, e, p, last_one):
                n_a, n_b = w.transposes(e, last_one)
                pipelined = not w.alone and not last_one
                if w.alone:
                    for m in range(SPLIT):
                        expert_low(w, e, p, m)
                    for h in range(2):
                        dve.wait_ge(w.tr_hi, e * 4 + (h + 1))
                        xe_low(w, h, bank[6 + h])
                for m in range(CPE):
                    if m == 3:
                        clamp(w, e, 0)
                    if m == 7:
                        dve.wait_ge(w.tr_hi, n_a + 1)
                        act_low(w, 0, bank[6])
                        clamp(w, e, 1)
                        if pipelined:
                            dve.wait_ge(w.tr_hi, n_a + 2)
                            xe_low(w, 0, bank[7])
                        activate(w, e, 1)
                    if m == 8:
                        dve.wait_ge(w.tr_hi, n_b + 1)
                        act_low(w, 1, bank[6] if pipelined else bank[7])
                    if m == 9 and pipelined:
                        dve.wait_ge(w.tr_hi, n_b + 2)
                        xe_low(w, 1, bank[7])
                    if (m + LOOK < CPE or pipelined) and (m + LOOK) % CPE in w.dve_chunks:
                        expert_low(w, e, p, m + LOOK)
                    if m == 3:
                        activate(w, e, 0)

            for h in range(2):
                dve.wait_ge(first.tr_hi, h + 1)
                xe_low(first, h, bank[6 + h])
            passes(dve, lambda e, p, last_one: expert(first, e, p, last_one))
            n = dve.value_load(n_extra[0:1, 0:1], min_val=0, max_val=MAX_EXTRA)
            with dve.If(n > 0):
                elink = linked(dve, extra_step)
                dve.wait_ge(extra_in, 16)
                elink(TTO(extra_on[:, :].rearrange("p (e b) -> p e b", b=NB), counts[:, :].unsqueeze(2).to_broadcast([1, E, NB]),
                          extra_cst[:, 0:P].rearrange("p (e b) -> p e b", b=NB), ALU.is_gt))
                elink(dve.tensor_tensor_scan(extra_sum[:, :], ones[0:1, :], extra_on[:, :], 0.0, ALU.mult, ALU.add))
                elink(TTO(extra_on[:, :], extra_on[:, :], iota[0:1, :], ALU.mult))
                elink(TTO(extra_eq[:, :, :], extra_sum[:, :].unsqueeze(1).to_broadcast([1, 16, P]),
                          extra_cst[:, P:P + 16].unsqueeze(2).to_broadcast([1, 16, P]), ALU.is_equal))
                elink(TTO(extra_eq[:, :, :], extra_eq[:, :, :], extra_on[:, :].unsqueeze(1).to_broadcast([1, 16, P]), ALU.mult))
                elink(dve.tensor_reduce(extra_f[:, :], extra_eq[:, :, :], AX.X, ALU.add))
                dve.tensor_copy(extra[:, :], extra_f[:, :]).then_inc(extra_ready, 1)
            dve.nop()
            with dve.Fori(0, MAX_EXTRA) as j:
                with dve.If(j < n):
                    expert(more, j, 0, False)
                dve.nop()
            elinks = linked(dve, end_step)
            dve.wait_ge(x_end_in, 16)
            dve.wait_ge(ln2_in, 32)
            for t in range(TT):
                r = res[t % 2]
                dve.wait_ge(end_first, t + 1)
                for k in range(1, TOPK):
                    ins = STT(r[:, :], y_rows[t % 2][:, k, :], gate_w[:, t, k:k + 1], r[:, :], ALU.mult, ALU.add)
                    if k < TOPK - 1:
                        elinks(ins)
                ins.then_inc(end_sum, 1)
                dve.wait_ge(end_sum, t + 1)
                elinks(STT(r[:, :], x_end[:, t, :], ALPHA, r[:, :], ALU.mult, ALU.add))
                for h in range(2):
                    elinks(dve.bn_stats(stats[:, t, 6 * h:6 * h + 6], r[:, 512 * h:512 * h + 512]))
                elinks(dve.bn_aggr(mean_var[:, t, :], stats[:, t, :]))
                TS(std[:, t:t + 1], mean_var[:, t, 1:2], LN_EPS, None, ALU.add).then_inc(end_var, 1)
                dve.wait_ge(end_std, t + 1)
                elinks(dve.reciprocal(std[:, t:t + 1], std[:, t:t + 1]))
                if t >= 2:
                    dve.wait_ge(out_done[t % 2], 16 * (t // 2))
                elinks(TS(ln_t[t % 2][:, :], r[:, :], mean_var[:, t, 0:1], std[:, t:t + 1], ALU.subtract, ALU.mult))
                TTO(ln_t[t % 2][:, :], ln_t[t % 2][:, :], ln2g[:, :], ALU.mult).then_inc(end_scaled, 1)

        @block.gpsimd
        def _(pool):
            pool.memset(scoreT[:, :, :], 0.0)
            pool.wait_ge(cst_in, 32)
            pool.tensor_copy(cst_b[:, :], cst_b_in[:, :])
            pool.wait_ge(gla_in, 96)
            pool.tensor_copy(level_mask[:, :, :], mask_in[:, :, :]).then_inc(pool_ready, 1)
            pool.wait_ge(pool_ready, 1)
            pool.memset(f_q[DH:DH + 1, :, :], 1.0).then_inc(pool_ready, 1)
            pool.wait_ge(pool_ready, 2)
            pool.memset(pool_idle[:, :], 0.0).then_inc(pool_ready, 1)
            pool.wait_ge(pool_ready, 3)
            pool.wait_ge(crow_ready, 1)
            for h in range(HEADS):
                pool.dma_start(f_k[DH:DH + 1, h, :], f_raw[h:h + 1, :]).then_inc(crow_in, 16)
            for t in range(TT):
                pool.wait_ge(scaled, t + 1)
                pool.tensor_tensor(x1[:, t, :], x1[:, t, :], ln_b[:, :], ALU.add).then_inc(x1_ready, 1)
            pool.wait_ge(used, N_MIX)
            pool.memset(x_rows[:, :], 0.0).then_inc(pool_ready, 1)
            pool.wait_ge(pool_ready, 4)
            pool.wait_ge(x1_out, 16 * TT)
            pool.wait_ge(route_ready, 1)

            def gather(w, n, col):
                pool.tensor_copy(gix_now[:, :], gather_ix[:, bass.ds(col, 1)]).then_inc(w.gix, 1)
                pool.wait_ge(w.gix, n)
                pool.tensor_tensor(pool_idle[:, :], pool_idle[:, :], pool_idle[:, :], ALU.add)
                pool.indirect_dma_start(x_rows[:, :], None, x1_dram, bass.IndirectOffsetOnAxis(ap=gix_now[:, 0:1], axis=0),
                                        bounds_check=T - 1, oob_is_err=False).then_inc(w.gathered, 16)

            def scatter(w, n, col):
                pool.tensor_copy(six_now[:, :], scatter_ix[:, bass.ds(col, 1)]).then_inc(w.six, 1)
                pool.wait_ge(w.six, n)
                pool.tensor_tensor(pool_idle[:, :], pool_idle[:, :], pool_idle[:, :], ALU.add)
                pool.indirect_dma_start(y_dram, bass.IndirectOffsetOnAxis(ap=six_now[:, 0:1], axis=0), y_sb[:, :], None,
                                        bounds_check=TOPK * T - 1, oob_is_err=False).then_inc(w.scattered, 16)

            def expert_low(w, e, p, m):
                pool.wait_ge(w.hi, e * CPE + (m + 1))
                pool.tensor_tensor(w_lo[m % 4][:, :], w.raw(p, m)[:, :], w_hi[m % 4][:, :].bitcast(F32), ALU.subtract)\
                    .then_inc(w.lo_pool, 1)

            def expert(e, p, last_one):
                if not last_one:
                    pool.wait_ge(first.tr, e * 4 + 2)
                    gather(first, e + 2, (e + 1) * NB)
                if not (isinstance(e, int) and e == 0):
                    pool.wait_ge(first.y_copied, e)
                    scatter(first, e, (e - 1) * NB)
                for m in POOL_CHUNKS:
                    expert_low(first, e, p, m)

            gather(first, 1, 0)
            passes(pool, expert)
            pool.wait_ge(first.y_copied, E)
            scatter(first, E, (E - 1) * NB)
            pool.wait_ge(first.scattered, 16 * E)
            n = pool.value_load(n_extra[0:1, 0:1], min_val=0, max_val=MAX_EXTRA)
            with pool.Fori(0, MAX_EXTRA) as j:
                with pool.If(j < n):
                    pool.wait_ge(extra_ready, 1)
                    col = pool.value_load(extra[0:1, bass.ds(j, 1)], min_val=0, max_val=P - 1)
                    gather(more, j + 1, col)
                    pool.wait_ge(more.y_copied, j + 1)
                    scatter(more, j + 1, col)
                    pool.wait_ge(more.scattered, (j + 1) * 16)
                    pool.nop()
                pool.nop()
            pool.memset(gix_now[:, :], 0).then_inc(experts_done, 1)
            for t in range(TT):
                pool.wait_ge(end_scaled, t + 1)
                pool.tensor_tensor(ln_t[t % 2][:, :], ln_t[t % 2][:, :], ln2b[:, :], ALU.add).then_inc(end_ready, 1)


def constants():
    import numpy as np

    r = np.arange(P)
    s, t = r[:, None], r[None, :]
    cf = np.zeros((P, 5 * P + 16), np.float32)
    cf[:, 0:P] = s == t
    cf[:, P:2 * P] = t
    cf[:, 2 * P:3 * P] = 1
    cf[:, 3 * P:3 * P + 16] = (np.arange(TOPK)[:, None] * T + np.arange(TT)[None, :] * P).reshape(1, 16) + s + 1
    cf[:, 3 * P + 16:] = (s // DK) == (np.arange(256)[None, :] // DH)
    cb = np.zeros((P, 4 * P + E), np.float32)
    cb[:, 0:P] = s == t
    cb[:, P:2 * P] = np.where(t <= s, 0.0, NEG)
    cb[:, 2 * P:3 * P] = s < t
    cb[:, 3 * P:4 * P] = 1
    cb[:96, 4 * P:] = (s[:96] % 32) == np.arange(E)[None, :]
    masks = np.zeros((P, 8, P), np.float32)
    for i, h in enumerate(LEVELS):
        masks[:, i, :] = (s // (2 * h) == t // (2 * h)) & (s % (2 * h) < h) & (t % (2 * h) >= h)
    masks[:, 7, :] = s == t
    extra = np.zeros((1, P + 16), np.float32)
    extra[0, :P] = np.where(r % NB, r % NB * P, 10 * T)
    extra[0, P:] = np.arange(16) + 1
    return cf, cb, masks, extra


def kernel(x, w_in, fox_fb, gla_a_up, gla_a_b, gla_norm_g, w_branch, w_out, ln1_g, ln1_b, w_router, b_router, w_gu, b_gu,
           w_dn, b_dn, ln2_g, ln2_b):
    import numpy as np
    import concourse.bacc as bacc
    from concourse.bass_utils import run_bass_kernel_spmd

    f32 = np.float32
    x, w_in, w_branch, w_out = (np.asarray(a)[0] for a in (x, w_in, w_branch, w_out))
    sizes = (256, 256, 256, 4, 128, 128, 256, 16, 256, 256, 256, 256, 3 * D)
    at = np.concatenate([[0], np.cumsum(sizes)])
    fq, fk, fv, ff, gq, gk, gv, ga, gr, mq, mk, mv, gt = (w_in[:, at[i]:at[i + 1]] for i in range(13))

    def by_tile(w):
        n = w.shape[1] // P
        c = w.reshape(KT, P, n, P).transpose(1, 2, 0, 3).reshape(P, n * D)
        return np.concatenate([c, np.zeros((P, CW - c.shape[1]), f32)], 1)

    def by_half(w):
        return list(w.reshape(2, 4, P, 512).transpose(0, 2, 1, 3).reshape(2, P, CW))

    small = np.concatenate([ga, np.zeros((D, 16), f32), ff, np.zeros((D, P - 36), f32)], 1)
    chunks = [by_tile(w) for w in (small, np.concatenate([gq, gk], 1), fq, fk, mq, mk)]
    chunks += by_half(np.concatenate([fv, gv], 1)) + by_half(np.concatenate([mv, gr], 1))
    g = gt.reshape(D, 3, KT, P).transpose(0, 2, 1, 3).reshape(D, 24, P)
    gate = [by_tile(g[:, 2 * i:2 * i + 2].reshape(D, 256)) for i in range(12)]
    u = w_branch.reshape(3, 2, P, KT // 2, 2, P).transpose(3, 2, 4, 0, 1, 5).reshape(KT // 2, P, 1536)
    u = np.concatenate([u, np.zeros((KT // 2, P, CW - 1536), f32)], 2)
    chunks += gate[0:6] + [u[0]] + gate[6:9] + [u[1]] + gate[9:12] + [u[2], u[3]]
    chunks += by_half(w_out[:, 0:512]) + by_half(w_out[:, 512:1024])
    wmix = np.stack(chunks)
    assert wmix.shape == (N_MIX, P, CW)
    gu = np.asarray(w_gu)[0].reshape(E, 4, 2, P, 2, 512, 2)
    dn = np.asarray(w_dn)[0].reshape(E, 4, 2, P, D)
    wexp = np.empty((E, CPE, P, CW), f32)
    wexp[:, 0:8] = gu.transpose(0, 4, 1, 3, 2, 6, 5).reshape(E, 8, P, CW)
    wexp[:, 8:12] = dn.transpose(0, 1, 3, 2, 4).reshape(E, 4, P, CW)
    b1 = np.asarray(b_gu)[0].reshape(E, 2, 512, 2).transpose(0, 1, 3, 2).reshape(E, 2 * D)
    b_moe = np.concatenate([b1, np.asarray(b_dn)[0]], 1)
    cf, cb, masks, extra = constants()
    arrays = {
        "xT": x.T.reshape(KT, P, T).transpose(1, 0, 2), "x": x.reshape(TT, P, D).transpose(1, 0, 2),
        "wmix": wmix, "wexp": wexp.reshape(E * CPE * P, CW),
        "a_up": np.asarray(gla_a_up)[0], "a_b": np.asarray(gla_a_b)[0].reshape(P, 1), "fb": np.asarray(fox_fb)[0].reshape(HEADS, 1),
        "norm_g": np.asarray(gla_norm_g)[0], "ln1_g": np.asarray(ln1_g)[0], "ln1_b": np.asarray(ln1_b)[0],
        "w_router": np.asarray(w_router)[0].reshape(KT, P, E).transpose(1, 0, 2), "b_router": np.asarray(b_router)[0],
        "b_moe": b_moe, "ln2_g": np.asarray(ln2_g)[0], "ln2_b": np.asarray(ln2_b)[0],
        "cf": cf, "cb": cb, "masks": masks, "extra_c": extra,
    }
    arrays = {n: np.ascontiguousarray(a) for n, a in arrays.items()}
    nc = bacc.Bacc("TRN2", target_bir_lowering=False, num_devices=1)
    ins = {n: nc.dram_tensor(f"in_{n}", a.shape, mybir.dt.from_np(a.dtype), kind="ExternalInput").ap()
           for n, a in arrays.items()}
    out = nc.dram_tensor("out", (T, D), mybir.dt.float32, kind="ExternalOutput").ap()
    build_kernel(nc, out=out, **ins)
    r = run_bass_kernel_spmd(nc, [{f"in_{n}": a for n, a in arrays.items()}], core_ids=[0])
    return r.results[0]["out"].reshape(1, T, D)
```

```python
from contextlib import ExitStack

import concourse.bass as bass
from concourse import mybir

D = 1024
T = 512
P = 128
KT = D // P
TT = T // P
HEADS = 4
DH = 64
DK = 32
E = 32
TOPK = 4
NB = T // P
ALPHA = 2.0 ** 0.25
LN_EPS = 1e-5
RMS_EPS = 1e-6
TAU = 16.0
LIMIT = 7.0
SWIGLU = 1.702
NEG = -1e30
MAX_EXTRA = (T * TOPK) // (P + 1)

CW = 2048
N_MIX = 30
CPE = 12
RAW_MIX = 4
RAW, SPLIT = 12, 4
PE_ROWS = 3
UNROLL = 2
LOOK = SPLIT
POOL_CHUNKS = (5, 10)

SMALL, GQ, GK, FQ, FK, TOK_A, MQ, MK, TOK_B = 0, 1, 2, 3, 5, 7, 11, 13, 15
GATE = 19
GATE_SLOTS = 12
W_GATES = [10 + g // 2 + (0 if g < 12 else (g - 8) // 4) for g in range(24)]
W_UP = [16 + 3 * (d // 2) for d in range(KT)]
W_OUT = 26
LEVELS = (64, 32, 16, 8, 4, 2, 1)


def chunk_of(mt):
    if mt < GATE:
        return (mt + 1) // 2, (mt + 1) % 2 if mt else 0
    return W_GATES[mt - GATE], (mt - GATE) % 2


def by_tokens(mt):
    return TOK_A <= mt < MQ or TOK_B <= mt < GATE


EARLY = [("mt", SMALL), ("mt", GQ), ("mt", GK), ("decay", 0), ("mt", FQ), ("mt", FQ + 1), ("mt", FK), ("level", 0),
         ("mt", FK + 1), ("level", 1), ("tok", 0), ("tok", 1), ("level", 2), ("tok", 2), ("tok", 3), ("level", 3),
         ("tok", 4), ("tok", 5), ("level", 4), ("tok", 6), ("tok", 7), ("level", 5), ("mt", MQ), ("level", 6),
         ("mt", MQ + 1), ("level", 7), ("mt", MK), ("mt", MK + 1), ("carry", 0), ("tok", 8), ("carry", 1), ("tok", 9),
         ("tok", 10), ("carry", 2)] + [("tok", n) for n in range(11, 16)]
POOL_MIX = range(11, 18)
UNITS = 2 * HEADS * TT
LATE = [("up", 0), ("up", 1)]
for q in range(3):
    LATE += [("gate", 12 + 4 * q + i) for i in range(4)] + [("up", 2 * q + 2), ("up", 2 * q + 3)]


def unit(u):
    branch, h, qt = u // (HEADS * TT), (u // TT) % HEADS, u % TT
    return branch, h, qt


def build_kernel(nc, xT, x, wmix, wexp, a_up, a_b, fb, norm_g, ln1_g, ln1_b, w_router, b_router, b_moe, ln2_g, ln2_b,
                 cf, cb, masks, extra_c, out):
    F32, F32R, BF16 = mybir.dt.float32, mybir.dt.float32r, mybir.dt.bfloat16
    I32, U32, U8 = mybir.dt.int32, mybir.dt.uint32, mybir.dt.uint8
    ALU = mybir.AluOpType
    ACT = mybir.ActivationFunctionType
    AX = mybir.AxisListType

    ctx = ExitStack()
    with ctx:
        BASE = -(-nc.sbuf_base // 64) * 64
        A0 = BASE
        B0 = A0 + 8 * 8192
        C0 = B0 + SPLIT * 16384
        D0 = C0 + 32768
        D1 = D0 + 18432
        K0 = D1 + 24576

        def at(name, shape, dt, offset):
            return nc.alloc_sbuf_tensor_at(name, shape, dt, offset=offset)

        small_at = [K0]

        def small(name, shape, dt):
            size = {F32: 4, I32: 4, U32: 4, BF16: 2, U8: 1}[dt]
            for n in shape[1:]:
                size *= n
            t = at(name, shape, dt, small_at[0])
            small_at[0] += -(-size // 32) * 32
            return t

        slots_at = [A0 + 8192 * s for s in range(8)] + [D1 + 8192, D1 + 16384, D0, D0 + 8192]
        raw = [at(f"raw{s}", [P, CW], F32, slots_at[s]) for s in range(RAW)]
        w_hi = [at(f"w_hi{s}", [P, CW], F32R, B0 + 16384 * s) for s in range(SPLIT)]
        w_lo = [at(f"w_lo{s}", [P, CW], F32R, B0 + 16384 * s + 8192) for s in range(SPLIT)]
        xT_hi = at("xT_hi", [P, KT, T], F32R, B0 + 32768)
        xT_lo = at("xT_lo", [P, KT, T], F32R, B0 + 49152)
        x1 = at("x1", [P, TT, D], F32, B0 + 32768)
        x1T = at("x1T", [P, KT, T], F32, B0 + 49152)
        G0 = A0 + 32768
        scoreT = at("scoreT", [P, HEADS, T], F32, G0)
        decay = at("decay", [P, T], F32, G0 + 8192)
        ratio = at("ratio", [P, T], F32, G0 + 10240)
        q_dec = [at(f"q_dec{i}", [P, T], F32, G0 + 12288 + 2048 * i) for i in range(2)]
        k_dec = [at(f"k_dec{i}", [P, T], F32, G0 + 16384 + 2048 * i) for i in range(2)]
        squares = at("squares", [P, 4 * 256], F32, G0 + 16384)
        k_end = at("k_end", [P, T], F32, G0 + 20480)
        k_endT = at("k_endT", [P, T], F32, G0 + 22528)
        state = at("state", [P, 3, 256], F32, G0 + 24576)
        y_gla = at("y_gla", [P, TT, 256], F32, G0 + 27648)
        norm_gb = at("norm_gb", [P, 256], F32, G0 + 31744)
        log1p = at("log1p", [P, T], F32, G0 + 22528)
        f_raw = at("f_raw", [HEADS, T], F32, G0 + 27648)
        f_log = at("f_log", [HEADS, T], F32, G0 + 29696)
        f_cum = at("f_cum", [HEADS, T], F32, G0 + 24576)
        ga_sb = at("ga_sb", [16, T], F32, G0 + 20480)
        probs = [at(f"probs{i}", [P, T], F32, G0 + 2048 * i) for i in range(2)]
        probsT = [at(f"probsT{i}", [P, T], F32, G0 + 4096 + 2048 * i) for i in range(2)]
        mix_acc = [at(f"mix_acc{i}", [P, T], F32, G0 + 2048 * i) for i in range(2)]
        mix_tmp = [at(f"mix_tmp{i}", [P, T], F32, G0 + 4096 + 2048 * i) for i in range(2)]
        gates = at("gates", [P, GATE_SLOTS, T], F32, G0 + 8192)
        f_q = at("f_q", [P, HEADS, T], F32, C0)
        f_k = at("f_k", [P, HEADS, T], F32, C0 + 8192)
        m_q = at("m_q", [P, 2, T], F32, C0 + 16384)
        m_k = at("m_k", [P, 2, T], F32, C0 + 20480)
        g_q = at("g_q", [P, T], F32, C0 + 24576)
        g_k = at("g_k", [P, T], F32, C0 + 26624)
        level_mask = at("level_mask", [P, 8, P], U8, C0 + 28672)
        head_mask = at("head_mask", [P, 256], F32, C0 + 29696)
        merged_hi = at("merged_hi", [P, KT, T], F32R, C0)
        merged_lo = at("merged_lo", [P, KT, T], F32R, C0 + 16384)
        values = at("values", [P, TT, D], F32, D0)
        mask_in = at("mask_in", [P, 8, P], F32, D0)
        cst_b_in = at("cst_b_in", [P, 4 * P + E], F32, D0 + 4096)
        bias_f = at("bias_f", [96, 3 * D], F32, D0)
        bias_parts = at("bias_parts", [96, 3 * D], BF16, D0 + 12288)
        xT_in = at("xT_in", [P, KT, T], F32, D1)
        yT_hi = at("yT_hi", [P, 6, T], F32R, D1)
        yT_lo = at("yT_lo", [P, 6, T], F32R, D1 + 12288)
        ln_g = at("ln_g", [P, D], F32, D1)
        ln_b = at("ln_b", [P, D], F32, D1 + 4096)
        x_tok = at("x_tok", [P, TT, D], F32, D1 + 8192)
        glu_g = at("glu_g", [P, 512], F32, C0)
        glu_u = at("glu_u", [P, 512], F32, C0 + 2048)
        glu_s = at("glu_s", [P, 512], F32, C0 + 4096)
        act = [at(f"act{h}", [P, 512], F32, C0 + 6144 + 2048 * h) for h in range(2)]
        y_sb = at("y_sb", [P, D], F32, C0 + 10240)
        x_rows = at("x_rows", [P, D], F32, C0 + 14336)
        xe_hi = at("xe_hi", [P, KT, P], F32R, C0 + 18432)
        xe_lo = at("xe_lo", [P, KT, P], F32R, C0 + 22528)
        bias3 = at("bias3", [96, 3 * D], BF16, C0 + 26624)
        aT_hi = [at(f"aT_hi{h}", [P, 4, P], F32R, D1 + 4096 * h) for h in range(2)]
        aT_lo = [at(f"aT_lo{h}", [P, 4, P], F32R, D1 + 4096 * h + 2048) for h in range(2)]
        y_rows = [at(f"y_rows{t}", [P, TOPK, D], F32, A0 + 16384 * t) for t in range(TT)]
        res = [at(f"res{t}", [P, D], F32, B0 + 4096 * t) for t in range(TT)]
        ln_t = [at(f"ln_t{t}", [P, D], F32, B0 + 16384 + 4096 * t) for t in range(TT)]
        x_end = at("x_end", [P, TT, D], F32, D1 + 8192)
        ln2g = at("ln2g", [P, D], F32, D0)
        gate_diag = at("gate_diag", [P, TT, PE_ROWS, P], F32, D0 + 12288)
        ln2b = at("ln2b", [P, D], F32, D0 + 4096)
        cst = small("cst", [P, 3 * P + 16], F32)
        ident = cst[:, 0:P]
        iota = cst[:, P:2 * P]
        ones = cst[:, 2 * P:3 * P]
        row_id = cst[:, 3 * P:3 * P + 16]
        cst_b = small("cst_b", [P, 4 * P + E], BF16)
        ident_b = cst_b[:, 0:P]
        causal = cst_b[:, P:2 * P]
        before = cst_b[:, 2 * P:3 * P]
        ones_b = cst_b[:, 3 * P:4 * P]
        pick = cst_b[0:96, 4 * P:4 * P + E]
        a_up_sb = small("a_up_sb", [16, P], F32)
        a_b_sb = small("a_b_sb", [P, 1], F32)
        fb_sb = small("fb_sb", [HEADS, 1], F32)
        b_r = small("b_r", [P, E], F32)
        scatter_ix = small("scatter_ix", [P, P], I32)
        gather_ix = small("gather_ix", [P, P], I32)
        gix_now = small("gix_now", [P, 1], I32)
        six_now = small("six_now", [P, 1], I32)
        pool_idle = small("pool_idle", [P, 1], F32)
        gate_w = small("gate_w", [P, TT, TOPK], F32)
        counts = small("counts", [1, E], F32)
        n_extra = small("n_extra", [1, 1], I32)
        extra = small("extra", [1, 16], I32)
        stats = small("stats", [P, TT, 12], F32)
        mean_var = small("mean_var", [P, TT, 2], F32)
        std = small("std", [P, TT], F32)
        shift = small("shift", [P, TT], F32)
        top_v = small("top_v", [P, TT, 8], F32)
        top_i = small("top_i", [P, TT, 8], U32)
        ix_f = small("ix_f", [P, TT, TOPK], F32)
        pos, blk, slot = (small(n, [P, TT * TOPK], F32) for n in ("pos", "blk", "slot"))
        exp4 = small("exp4", [P, TT, TOPK], F32)
        exp_sum = small("exp_sum", [P, TT], F32)
        row_max = small("row_max", [P, 2], F32)
        row_sum = small("row_sum", [P, 2], F32)
        row_inv = small("row_inv", [P, 2], F32)
        rms = small("rms", [P, 4 * HEADS], F32)
        end_dec = small("end_dec", [P, TT], F32)
        assert small_at[0] <= nc.sbuf_usable_end, (small_at[0], nc.sbuf_usable_end)
        w_r = at("w_r", [P, KT, E], F32, C0 + 18432)
        onehot_s = at("onehot_s", [P, TT * TOPK, P], F32R, C0)
        onehot_c = at("onehot_c", [P, TT * TOPK, P], F32R, D1)
        table = at("table", [P, P], F32, C0 + 19456)
        wrap = at("wrap", [P, P], F32, C0 + 19968)
        wrapped = at("wrapped", [P, P], F32, C0 + 20480)
        logits = at("logits", [P, TT, E], F32, C0 + 20992)
        hits = at("hits", [P, TT, E], BF16, C0 + 21504)
        junk = at("junk", [P, E], F32, C0 + 21760)
        over = at("over", [1, E], F32, C0 + 21888)
        chosen = at("chosen", [P, TT, TOPK, E], F32, C0 + 10240)
        places_of = at("places_of", [P, TT, TOPK, E], F32, C0 + 12288)
        blk_is = at("blk_is", [P, TT * TOPK, NB], F32, C0 + 22016)
        row_of = at("row_of", [P, TT, TOPK, E], F32, C0 + 8192)
        extra_on = at("extra_on", [1, P], F32, A0 + 32768)
        extra_sum = at("extra_sum", [1, P], F32, A0 + 33280)
        extra_eq = at("extra_eq", [1, 16, P], F32, A0 + 33792)
        extra_f = at("extra_f", [1, 16], F32, A0 + 41984)
        extra_cst = at("extra_cst", [1, P + 16], F32, A0 + 42048)

        bank = [ctx.enter_context(nc.psum_tensor(f"bank{i}", [P, 512], F32)) for i in range(8)]
        x1_dram = nc.dram_tensor("x1_scratch", (T, D), F32, kind="Internal").ap()
        y_dram = nc.dram_tensor("y_scratch", (TOPK * T, D), F32, kind="Internal").ap()

        def sem(name):
            return ctx.enter_context(nc.semaphore(name))

        x_in = [sem(f"x_in{h}") for h in range(4)]
        cst_in, gla_in, crow_in, bias_in, tok_in, w_r_in, x1_out = (
            sem(n) for n in ("cst_in", "gla_in", "crow_in", "bias_in", "tok_in", "w_r_in", "x1_out"))
        mix_in = [sem(f"mix_in{s}") for s in range(RAW_MIX)]
        ln2_in, x_end_in, y_in, out_done = sem("ln2_in"), sem("x_end_in"), [sem(f"y_in{t}") for t in range(TT)], sem("out_done")
        m_hi, m_lo, x_hi, x_lo = sem("m_hi"), sem("m_lo"), sem("x_hi"), sem("x_lo")
        used, first_tile, token_tile, proj_read = sem("used"), sem("first_tile"), sem("token_tile"), sem("proj_read")
        pool_ready = sem("pool_ready")
        decay_pre, log_ready, diff_ready, ratio_ready, qk_ready = (
            sem(n) for n in ("decay_pre", "log_ready", "diff_ready", "ratio_ready", "qk_ready"))
        level_done, level_read, crow_ready = sem("level_done"), sem("level_read"), sem("crow_ready")
        carry_pe, carry_act, carry_dve, y_scaled = sem("carry_pe"), sem("carry_act"), sem("carry_dve"), sem("y_scaled")
        score_done, max_ready, exp_done, norm_done, pT_done, pT_read, pv_done = (sem(n) for n in (
            "score_done", "max_ready", "exp_done", "norm_done", "pT_done", "pT_read", "pv_done"))
        yT_hi_ready, yT_lo_ready = sem("yT_hi_ready"), sem("yT_lo_ready")
        gate_sig, up_done, up_read, merged_ready, merged_hi_ready, merged_lo_ready, bias_split, bias_ready = (sem(n) for n in (
            "gate_sig", "up_done", "up_read", "merged_ready", "merged_hi_ready", "merged_lo_ready", "bias_split", "bias_ready"))
        out_tile, var_ready, std_ready, shift_ready, normed, scaled, x1_ready, x1T_done, x1T_read = (sem(n) for n in (
            "out_tile", "var_ready", "std_ready", "shift_ready", "normed", "scaled", "x1_ready", "x1T_done", "x1T_read"))
        logit_done, top_ready, gate_exp, hits_ready, pos_done, onehot_ready, onehot_used, counted, route_ready = (
            sem(n) for n in ("logit_done", "top_ready", "gate_exp", "hits_ready", "pos_done", "onehot_ready", "onehot_used",
                             "counted", "route_ready"))
        dve_step, act_step, bias_step = sem("dve_step"), sem("act_step"), sem("bias_step")
        extra_in, extra_step, extra_ready = sem("extra_in"), sem("extra_step"), sem("extra_ready")
        end_step, slot_ready, rows_ready, diag_ready = (sem(n) for n in ("end_step", "slot_ready", "rows_ready", "diag_ready"))
        experts_done, x_scaled, last_row, with_x, end_first, end_var, end_std, end_shift, end_normed, end_scaled = (
            sem(n) for n in ("experts_done", "x_scaled", "last_row", "with_x", "end_first", "end_var", "end_std", "end_shift",
                             "end_normed", "end_scaled"))
        end_ready, last_ready = sem("end_ready"), sem("last_ready")

        class Pass:

            def __init__(self, tag, slots, alone):
                self.alone, self.slots = alone, slots
                self.raw_in = [sem(f"{tag}_raw_in{s}") for s in range(slots)]
                self.hi, self.lo_dve, self.lo_pool, self.used = (
                    sem(f"{tag}_{n}") for n in ("hi", "lo_dve", "lo_pool", "used"))
                self.tr, self.tr_hi, self.tr_lo = sem(f"{tag}_tr"), sem(f"{tag}_tr_hi"), sem(f"{tag}_tr_lo")
                self.glu_read, self.sig, self.gated, self.act_ready = (
                    sem(f"{tag}_{n}") for n in ("glu_read", "sig", "gated", "act_ready"))
                self.y_copied, self.gathered, self.scattered = (
                    sem(f"{tag}_{n}") for n in ("y_copied", "gathered", "scattered"))
                self.gix, self.six = sem(f"{tag}_gix"), sem(f"{tag}_six")
                self.dve_chunks = [m for m in range(CPE) if alone or m not in POOL_CHUNKS]

            def wait_lo(self, eng, e, m):
                e, m = e + m // CPE, m % CPE
                if m in self.dve_chunks:
                    n = len(self.dve_chunks)
                    eng.wait_ge(self.lo_dve, e * n + (self.dve_chunks.index(m) + 1))
                else:
                    eng.wait_ge(self.lo_pool, e * len(POOL_CHUNKS) + (POOL_CHUNKS.index(m) + 1))

            def wait_raw(self, eng, e, p, m):
                if self.alone:
                    eng.wait_ge(self.raw_in[m % self.slots], (e * (CPE // self.slots) + m // self.slots + 1) * 16)
                else:
                    c = p * CPE + m
                    eng.wait_ge(self.raw_in[c % self.slots], ((e - p) * CPE // RAW + c // self.slots + 1) * 16)

            def raw(self, p, m):
                return raw[m % self.slots] if self.alone else raw[(p * CPE + m) % self.slots]

            def transposes(self, e, last):
                return (e * 4 + 2, e * 4 + 3) if self.alone or last else (e * 4 + 2, e * 4 + 4)

        first, more = Pass("first", RAW, False), Pass("more", SPLIT, True)
        block = ctx.enter_context(nc.Block())

        def linked(eng, s):
            count = [0]

            def link(ins):
                count[0] += 1
                ins.then_inc(s, 1)
                eng.wait_ge(s, count[0])
            return link

        def tile_done(mt):
            if by_tokens(mt):
                b, t = (0, mt - TOK_A) if mt < MQ else (1, mt - TOK_B)
                return (used, (6, 10)[b]) if t == TT - 1 else (token_tile, b * (TT - 1) + t + 1)
            c, j = chunk_of(mt)
            if j == 0 and mt != SMALL:
                return first_tile, c if mt < TOK_A else c - 2 if mt < GATE else 6 + (mt - GATE) // 2
            return used, c + 1

        def up_signal(i):
            return (used, W_UP[i // 3] + 1) if i % 6 == 5 else (up_done, i - i // 6 + 1)

        def freed(kind, n):
            if kind in ("mt", "gate"):
                c, j = chunk_of(n if kind == "mt" else GATE + n)
                return c if j == 1 or c == 0 else None
            if kind == "tok":
                return (4, 5, 8, 9)[n // TT] if n % TT == TT - 1 else None
            if kind == "up":
                return W_UP[n] if n % 2 else None
            return W_OUT + n if kind == "out" else None

        HALF = TT * TOPK // 2

        def block_rows(eng, i):
            n = slice(i * HALF, i * HALF + HALF)
            shape = [P, HALF, E, NB]
            return eng.tensor_tensor(onehot_c[:, n, :].rearrange("p n (e b) -> p n e b", b=NB),
                                     row_of[:, :, :, :].rearrange("p t k e -> p (t k) e")[:, n, :].unsqueeze(3).to_broadcast(shape),
                                     blk_is[:, n, :].unsqueeze(2).to_broadcast(shape), ALU.mult)

        def fill(s):
            return GATE + s // 3, (range(0, 3), range(3, 6), range(6, 8))[s % 3]

        FILL_STEPS = 36
        turns = E // UNROLL

        def passes(eng, body):
            for p in range(UNROLL):
                body(p, p, p == UNROLL - 1 and turns == 1)
            with eng.Fori(1, turns - 1) as i:
                for p in range(UNROLL):
                    body(i * UNROLL + p, p, False)
            for p in range(UNROLL):
                body(E - UNROLL + p, p, p == UNROLL - 1)

        @block.sync
        def _(sp):
            sp.dma_start(raw[0][:, 0:D], wmix[0][:, 0:D]).then_inc(mix_in[0], 16)
            for h in range(4):
                sp.dma_start(xT_in[:, 2 * h:2 * h + 2, :], xT[:, 2 * h:2 * h + 2, :]).then_inc(x_in[h], 16)
            for c in range(1, N_MIX):
                s = c % RAW_MIX
                if c >= RAW_MIX:
                    sp.wait_ge(m_lo, c - RAW_MIX + 1)
                sp.dma_start(raw[s][:, :], wmix[c]).then_inc(mix_in[s], 16)
                if c == 1:
                    for to, src in ((cst[:, :], cf[:, 0:3 * P + 16]), (cst_b_in[:, :], cb)):
                        sp.dma_start(to, src).then_inc(cst_in, 16)
                    for to, src in ((a_up_sb[:, :], a_up), (a_b_sb[:, :], a_b), (fb_sb[:, :], fb),
                                    (mask_in[:, :, :], masks), (head_mask[:, :], cf[:, 3 * P + 16:5 * P + 16]),
                                    (norm_gb[:, :], norm_g.partition_broadcast(P))):
                        sp.dma_start(to, src).then_inc(gla_in, 16)
                if c == 19:
                    sp.wait_ge(pv_done, UNITS)
                    for q in range(3):
                        sp.dma_start(bias_f[32 * q:32 * q + 32, :], b_moe).then_inc(bias_in, 16)
            sp.wait_ge(used, W_UP[-1] + 1)
            for to, src in ((x_tok[:, :, :], x), (ln_g[:, :], ln1_g.partition_broadcast(P)),
                            (ln_b[:, :], ln1_b.partition_broadcast(P)), (b_r[:, :], b_router.partition_broadcast(P))):
                sp.dma_start(to, src).then_inc(tok_in, 16)
            sp.wait_ge(merged_lo_ready, KT)
            for c in (4, 5, 6, 7):
                sp.dma_start(raw[c][:, :], wexp[c * P:(c + 1) * P, :]).then_inc(first.raw_in[c], 16)
            sp.wait_ge(m_lo, N_MIX)
            for c in (0, 1, 2, 3):
                sp.dma_start(raw[c][:, :], wexp[c * P:(c + 1) * P, :]).then_inc(first.raw_in[c], 16)
            sp.wait_ge(used, N_MIX)
            sp.dma_start(w_r[:, :, :], w_router).then_inc(w_r_in, 16)
            for t in range(TT):
                sp.wait_ge(x1_ready, t + 1)
                sp.dma_start(x1_dram[t * P:(t + 1) * P, :], x1[:, t, :]).then_inc(x1_out, 16)
            sp.wait_ge(var_ready, TT)
            sp.wait_ge(bias_split, 1)
            for c in (8, 9, 10):
                sp.dma_start(raw[c][:, :], wexp[c * P:(c + 1) * P, :]).then_inc(first.raw_in[c], 16)
            sp.wait_ge(bias_ready, 1)
            sp.dma_start(raw[11][:, :], wexp[11 * P:12 * P, :]).then_inc(first.raw_in[11], 16)
            for c in range(RAW, CPE * UNROLL):
                first.wait_lo(sp, 0, c - RAW)
                sp.dma_start(raw[c % RAW][:, :], wexp[c * P:(c + 1) * P, :]).then_inc(first.raw_in[c % RAW], 16)
            with sp.Fori(1, turns) as i:
                for c in range(CPE * UNROLL):
                    first.wait_lo(sp, i * UNROLL + (c - RAW) // CPE, (c - RAW) % CPE)
                    sp.dma_start(raw[c % RAW][:, :], wexp[bass.ds((i * (CPE * UNROLL) + c) * P, P), :])\
                      .then_inc(first.raw_in[c % RAW], 16)
            first.wait_lo(sp, E - 1, 9)
            sp.wait_ge(x1_out, 16 * TT)
            sp.dma_start(x_end[:, :, :], x1_dram.rearrange("(a p) n -> p a n", p=P)).then_inc(x_end_in, 16)
            first.wait_lo(sp, E - 1, 10)
            for to, src in ((ln2g[:, :], ln2_g), (ln2b[:, :], ln2_b)):
                sp.dma_start(to, src.partition_broadcast(P)).then_inc(ln2_in, 16)
            sp.wait_ge(route_ready, 2)
            n = sp.value_load(n_extra[0:1, 0:1], min_val=0, max_val=MAX_EXTRA)
            with sp.If(n > 0):
                sp.wait_ge(first.scattered, 16 * E)
                sp.dma_start(extra_cst[:, :], extra_c).then_inc(extra_in, 16)
                with sp.Fori(0, MAX_EXTRA) as j:
                    with sp.If(j < n):
                        sp.wait_ge(extra_ready, 1)
                        col = sp.value_load(extra[0:1, bass.ds(j, 1)], min_val=0, max_val=P - 1)
                        sp.wait_ge(more.gathered, (j + 1) * 16)
                        for m in range(CPE):
                            if m >= SPLIT:
                                sp.wait_ge(more.lo_dve, j * CPE + (m - SPLIT + 1))
                            sp.dma_start(raw[m % SPLIT][:, :], wexp[bass.ds(((col // NB) * CPE + m) * P, P), :])\
                              .then_inc(more.raw_in[m % SPLIT], 16)
                    sp.nop()
            sp.nop()
            sp.wait_ge(experts_done, 1)
            y_by_tile = y_dram.rearrange("(k a p) n -> a p k n", k=TOPK, p=P)
            for t in range(TT):
                sp.dma_start(y_rows[t][:, :, :], y_by_tile[t]).then_inc(y_in[t], 16)
            for t in range(TT):
                sp.wait_ge(*((end_ready, t + 1) if t < TT - 1 else (last_ready, 1)))
                sp.dma_start(out[t * P:(t + 1) * P, :], ln_t[t][:, :]).then_inc(out_done, 16)
            sp.wait_ge(out_done, 16 * TT)

        @block.tensor
        def _(pe):
            def split3(dst, lh, ll, rh, rl, start, stop):
                pe.matmul(dst, lh, rh, start=start, stop=False)
                pe.matmul(dst, lh, rl, start=False, stop=False)
                return pe.matmul(dst, ll, rh, start=False, stop=stop)

            def transpose(dst, src):
                return pe.matmul(dst, src, ident, is_transpose=True, start=True, stop=True)

            def weights(c):
                pe.wait_ge(m_hi, c + 1)
                pe.wait_ge(m_lo, c + 1)

            def columns(mt, ks=range(KT)):
                c, j = chunk_of(mt)
                if ks[0] == 0:
                    weights(c)
                    if mt >= 4:
                        pe.wait_ge(proj_read, mt - 3)
                for k in ks:
                    if mt == SMALL:
                        pe.wait_ge(x_lo, k // 2 + 1)
                    o = (j * KT + k) * P
                    last = split3(bank[mt % 4][:, :], w_hi[c % 2][:, o:o + P], w_lo[c % 2][:, o:o + P],
                                  xT_hi[:, k, :], xT_lo[:, k, :], k == 0, k == KT - 1)
                if ks[-1] == KT - 1:
                    last.then_inc(used if j == 1 or mt == SMALL else first_tile, 1)

            def tokens(n):
                half, t = n // TT % 2, n % TT
                c = (4, 5, 8, 9)[n // TT]
                mt = (TOK_A if n < 2 * TT else TOK_B) + t
                if t == 0:
                    weights(c)
                if half == 0:
                    pe.wait_ge(proj_read, mt - 3)
                for k in range(4):
                    kk = half * 4 + k
                    last = split3(bank[mt % 4][:, :], xT_hi[:, kk, t * P:(t + 1) * P], xT_lo[:, kk, t * P:(t + 1) * P],
                                  w_hi[c % 2][:, k * 512:(k + 1) * 512], w_lo[c % 2][:, k * 512:(k + 1) * 512],
                                  kk == 0, kk == KT - 1)
                if t == TT - 1:
                    last.then_inc(used, 1)
                elif half == 1:
                    last.then_inc(token_tile, 1)

            def level(n):
                pe.wait_ge(qk_ready, min(n, 6) + 1)
                if n >= 1:
                    pe.wait_ge(level_read, n)
                q, k = (q_dec[n % 2], k_dec[n % 2]) if n < 7 else (g_q, g_k)
                for h in range(HEADS):
                    for t in range(TT):
                        last = pe.matmul(bank[4 + h][:, t * P:(t + 1) * P], k[DK * h:DK * h + DK, t * P:(t + 1) * P],
                                         q[DK * h:DK * h + DK, t * P:(t + 1) * P], start=True, stop=True)
                last.then_inc(level_done, 1)

            def carry(n):
                if n == 0:
                    pe.wait_ge(carry_dve, 1)
                    pe.wait_ge(level_read, 8)
                    for t in range(TT):
                        last = transpose(bank[5][:, t * P:(t + 1) * P], k_end[:, t * P:(t + 1) * P])
                elif n == 1:
                    pe.wait_ge(carry_act, 1)
                    pe.wait_ge(proj_read, MQ)
                    for t in range(3):
                        last = pe.matmul(bank[6 + t // 2][:, (t % 2) * 256:(t % 2) * 256 + 256],
                                         k_endT[:, t * P:(t + 1) * P], values[:, t, 256:512], start=True, stop=True)
                elif n == 2:
                    pe.wait_ge(carry_dve, 2)
                    for t in range(TT):
                        o = bank[4 + t // 2][:, (t % 2) * 256:(t % 2) * 256 + 256]
                        if t > 0:
                            pe.matmul(o, q_dec[1][:, t * P:(t + 1) * P], state[:, t - 1, :], start=True, stop=True)
                        for h in range(HEADS):
                            last = pe.matmul(o[:, DH * h:DH * h + DH], scoreT[:, h, t * P:(t + 1) * P],
                                             values[:, t, 256 + DH * h:256 + DH * h + DH], start=t == 0, stop=True,
                                             skip_group_check=True)
                else:
                    pe.wait_ge(carry_dve, 4)
                    for i in range(2):
                        for t in range(TT):
                            last = transpose(bank[6 + i][:, t * P:(t + 1) * P], y_gla[:, t, i * P:(i + 1) * P])
                last.then_inc(carry_pe, 1)

            for kind, n in EARLY:
                if kind == "mt":
                    columns(n)
                elif kind == "tok":
                    tokens(n)
                elif kind == "level":
                    level(n)
                elif kind == "carry":
                    carry(n)
                else:
                    pe.wait_ge(cst_in, 32)
                    pe.wait_ge(gla_in, 96)
                    pe.wait_ge(proj_read, 1)
                    pe.matmul(bank[4][:, :], a_up_sb[:, :], ga_sb[:, :], start=True, stop=True).then_inc(decay_pre, 1)

            pe.wait_ge(crow_in, 16 * HEADS)
            pe.wait_ge(pool_ready, 2)
            pe.wait_ge(y_scaled, 1)
            for s in range(FILL_STEPS):
                if s == 1:
                    carry(3)
                if s < UNITS:
                    branch, h, qt = unit(s)
                    if s >= 2:
                        pe.wait_ge(exp_done, s - 1)
                    n = (qt + 1) * P
                    a = h % 2 * DH
                    q, k = (f_q[0:DH + 1, h, :], f_k[0:DH + 1, h, :]) if branch == 0 else (
                        m_q[a:a + DH, h // 2, :], m_k[a:a + DH, h // 2, :])
                    pe.matmul(bank[4 + s % 2][:, 0:n], q[:, qt * P:(qt + 1) * P], k[:, 0:n], start=True, stop=True)
                    pe.matmul(bank[4 + s % 2][:, qt * P:n], ident_b, causal, start=False, stop=True,
                              skip_group_check=True).then_inc(score_done, 1)
                if s == 1:
                    columns(*fill(s))
                    pe.wait_ge(yT_lo_ready, 2)
                if 1 <= s <= UNITS:
                    u = s - 1
                    pe.wait_ge(norm_done, u + 1)
                    pe.wait_ge(pT_read, u)
                    for kt in range(unit(u)[2] + 1):
                        last = transpose(bank[6][:, kt * P:(kt + 1) * P], probs[u % 2][:, kt * P:(kt + 1) * P])
                    last.then_inc(pT_done, 1)
                if s != 1:
                    columns(*fill(s))
                if 2 <= s < UNITS + 2:
                    u = s - 2
                    branch, h, qt = unit(u)
                    pe.wait_ge(pT_read, u + 1)
                    if u % 8 == 0 and u:
                        pe.wait_ge(yT_lo_ready, 2 + u // 8)
                    col = 512 * branch + DH * h
                    a = h % 2 * DH
                    for kt in range(qt + 1):
                        last = pe.matmul(bank[7][a:a + DH, qt * P:(qt + 1) * P], values[:, kt, col:col + DH],
                                         probsT[u % 2][:, kt * P:(kt + 1) * P], start=kt == 0, stop=kt == qt)
                    last.then_inc(pv_done, 1)

            for kind, n in LATE:
                if kind == "gate":
                    columns(GATE + n)
                    continue
                c = W_UP[n]
                weights(c)
                if n == 0:
                    pe.wait_ge(yT_lo_ready, 6)
                for b in range(3):
                    i = 3 * n + b
                    if i >= 4:
                        pe.wait_ge(up_read, i - 3)
                    for ct in range(2):
                        o = ((n % 2 * 3 + b) * 2 + ct) * P
                        y = (0, 2, 4)[b] + ct
                        last = split3(bank[4 + i % 4][:, :], w_hi[c % 2][:, o:o + P], w_lo[c % 2][:, o:o + P],
                                      yT_hi[:, y, :], yT_lo[:, y, :], ct == 0, ct == 1)
                    last.then_inc(up_signal(i)[0], 1)
            for n in range(4):
                weights(W_OUT + n)
                if n == 0:
                    pe.wait_ge(proj_read, GATE + 24)
                if n == 2:
                    pe.wait_ge(up_read, 3 * KT)
                for t in range(TT):
                    for k in range(4):
                        kk = n % 2 * 4 + k
                        pe.wait_ge(merged_lo_ready, kk + 1)
                        last = split3(bank[n // 2 * 4 + t][:, :],
                                      merged_hi[:, kk, t * P:(t + 1) * P], merged_lo[:, kk, t * P:(t + 1) * P],
                                      w_hi[n % 2][:, k * 512:(k + 1) * 512], w_lo[n % 2][:, k * 512:(k + 1) * 512],
                                      kk == 0, kk == KT - 1)
                    last.then_inc(used if t == TT - 1 else out_tile, 1)

            def x1_transposes(t):
                pe.wait_ge(x1_ready, t + 1)
                for h in range(2):
                    n = 2 * t + h
                    if n >= 4:
                        pe.wait_ge(x1T_read, n - 3)
                    for k in range(4):
                        last = transpose(bank[n % 4][:, k * P:(k + 1) * P], x1[:, t, (4 * h + k) * P:(4 * h + k + 1) * P])
                    last.then_inc(x1T_done, 1)

            def router(t):
                pe.wait_ge(x1T_read, 2 * t + 2)
                for k in range(KT):
                    last = pe.matmul(bank[4 if t < TT - 1 else 7][:, t * E:(t + 1) * E], x1T[:, k, t * P:(t + 1) * P],
                                     w_r[:, k, :], start=k == 0, stop=k == KT - 1)
                if t >= TT - 2:
                    last.then_inc(logit_done, 1)

            pe.wait_ge(w_r_in, 16)
            x1_transposes(0)
            x1_transposes(1)
            router(0)
            for t in range(2, TT):
                x1_transposes(t)
                router(t - 1)
            router(TT - 1)
            pe.wait_ge(hits_ready, 1)
            for t in range(TT):
                for a in range(t + 1):
                    last = pe.matmul(bank[5][:, t * E:(t + 1) * E], before if a == t else ones_b, hits[:, a, :],
                                     start=a == 0, stop=a == t)
            last.then_inc(pos_done, 1)
            for a in range(TT):
                last = pe.matmul(bank[7][:, 0:E], ones_b, hits[:, a, :], start=a == 0, stop=a == TT - 1)
            last.then_inc(counted, 1)
            for n in range(TT * TOPK):
                if n % HALF == 0:
                    pe.wait_ge(onehot_ready, n // HALF + 1)
                    if n:
                        pe.wait_ge(rows_ready, 1)
                last = pe.matmul(bank[6][:, 0:P], onehot_s[:, n, :], onehot_c[:, n, :], start=n == 0, stop=n == TT * TOPK - 1)
            last.then_inc(onehot_used, 1)

            def transposes4(w, dst, src, o):
                for k in range(4):
                    last = transpose(dst[:, k * P:(k + 1) * P], src[:, o + k * P:o + (k + 1) * P])
                last.then_inc(w.tr, 1)

            def expert(w, e, expert_no, last_one):
                w_ready = lambda m: (pe.wait_ge(w.hi, e * CPE + (m + 1)), w.wait_lo(pe, e, m))
                n_a, n_b = w.transposes(e, last_one)
                if w.alone:
                    pe.wait_ge(w.gathered, (e + 1) * 16)
                    for h in range(2):
                        transposes4(w, bank[6 + h], x_rows, 512 * h)
                pe.wait_ge(w.tr_hi, e * 4 + 2)
                pe.wait_ge(w.tr_lo, e * 4 + 2)
                for half in range(2):
                    banks = (bank[2 * half], bank[2 * half + 1])
                    if not w.alone and not (isinstance(e, int) and e == 0):
                        pe.wait_ge(w.glu_read, e * 2 + (half - 1))
                    for kp in range(4):
                        m = 4 * half + kp
                        if m == 6:
                            pe.wait_ge(w.act_ready, e * 2 + 1)
                            pe.wait_ge(w.tr_lo, n_a - 1)
                            transposes4(w, bank[6], act[0], 0)
                        w_ready(m)
                        if kp == 3:
                            for b in range(2):
                                o = (2 * half + b) * 512
                                pe.matmul(banks[b][:, :], pick[:, bass.ds(expert_no, 1)].to_broadcast([96, P]),
                                          bias3[:, o:o + 512], start=False, stop=False)
                        for k2 in range(2):
                            k = 2 * kp + k2
                            cols = [slice(k2 * D + 512 * b, k2 * D + 512 * b + 512) for b in range(2)]
                            for b in range(2):
                                pe.matmul(banks[b][:, :], xe_hi[:, k, :], w_hi[m % 4][:, cols[b]], start=k == 0, stop=False)
                                pe.matmul(banks[b][:, :], xe_hi[:, k, :], w_lo[m % 4][:, cols[b]], start=False, stop=False)
                            for b in range(2):
                                last = pe.matmul(banks[b][:, :], xe_lo[:, k, :], w_hi[m % 4][:, cols[b]], start=False,
                                                 stop=k == KT - 1)
                        last.then_inc(w.used, 1)
                pipelined = not w.alone and not last_one
                if pipelined:
                    pe.wait_ge(w.gathered, (e + 2) * 16)
                    pe.wait_ge(w.tr_lo, n_a)
                    transposes4(w, bank[7], x_rows, 0)
                if not w.alone and not (isinstance(e, int) and e == 0):
                    pe.wait_ge(w.y_copied, e)
                for q in range(4):
                    m = 8 + q
                    if q == 0:
                        pe.wait_ge(w.tr_lo, n_a + 1)
                    if q == 2:
                        pe.wait_ge(w.act_ready, e * 2 + 2)
                        pe.wait_ge(w.tr_lo, n_b - 1)
                        transposes4(w, bank[6] if pipelined else bank[7], act[1], 0)
                        if pipelined:
                            pe.wait_ge(w.tr_lo, n_b)
                            transposes4(w, bank[7], x_rows, 512)
                        pe.wait_ge(w.tr_lo, n_b + 1)
                    w_ready(m)
                    if q == 3:
                        for b in range(2):
                            o = 2 * D + 512 * b
                            pe.matmul(bank[4 + b][:, :], pick[:, bass.ds(expert_no, 1)].to_broadcast([96, P]),
                                      bias3[:, o:o + 512], start=False, stop=False)
                    for k2 in range(2):
                        k = 2 * q + k2
                        ah, al = aT_hi[k // 4][:, k % 4, :], aT_lo[k // 4][:, k % 4, :]
                        cols = [slice(k2 * D + 512 * b, k2 * D + 512 * b + 512) for b in range(2)]
                        for b in range(2):
                            pe.matmul(bank[4 + b][:, :], ah, w_hi[m % 4][:, cols[b]], start=k == 0, stop=False)
                            pe.matmul(bank[4 + b][:, :], ah, w_lo[m % 4][:, cols[b]], start=False, stop=False)
                        for b in range(2):
                            last = pe.matmul(bank[4 + b][:, :], al, w_hi[m % 4][:, cols[b]], start=False, stop=k == KT - 1)
                    last.then_inc(w.used, 1)

            pe.wait_ge(route_ready, 2)
            pe.wait_ge(bias_ready, 1)
            pe.wait_ge(first.gathered, 16)
            for h in range(2):
                transposes4(first, bank[6 + h], x_rows, 512 * h)
            passes(pe, lambda e, p, last_one: expert(first, e, e, last_one))
            n = pe.value_load(n_extra[0:1, 0:1], min_val=0, max_val=MAX_EXTRA)
            with pe.If(n > 0):
                with pe.Fori(0, MAX_EXTRA) as j:
                    with pe.If(j < n):
                        pe.wait_ge(extra_ready, 1)
                        col = pe.value_load(extra[0:1, bass.ds(j, 1)], min_val=0, max_val=P - 1)
                        expert(more, j, col // NB, False)
                    pe.nop()
            pe.nop()
            pe.wait_ge(diag_ready, 1)
            for t in range(TT):
                pe.wait_ge(y_in[t], 16)
                for h in range(2):
                    for k in range(PE_ROWS):
                        last = pe.matmul(bank[2 * t + h][:, :], gate_diag[:, t, k, :], y_rows[t][:, k, 512 * h:512 * h + 512],
                                         start=k == 0, stop=k == PE_ROWS - 1)
                    last.then_inc(end_first, 1)

        @block.scalar
        def _(act_e):
            link = linked(act_e, act_step)
            A = act_e.activation

            def high(c):
                act_e.wait_ge(mix_in[c % RAW_MIX], 16 * (c // RAW_MIX + 1))
                if c >= 2:
                    act_e.wait_ge(used, c - 1)
                n = D if c == 0 else CW
                A(w_hi[c % 2][:, 0:n], raw[c % RAW_MIX][:, 0:n], ACT.Copy).then_inc(m_hi, 1)

            def after(kind, n):
                c = freed(kind, n)
                if c is not None and c + 2 < N_MIX:
                    high(c + 2)

            def copy_out(mt):
                act_e.wait_ge(*tile_done(mt))
                if mt == TOK_A:
                    act_e.wait_ge(pool_ready, 1)
                b = bank[mt % 4]
                if mt == SMALL:
                    A(ga_sb[:, :], b[0:16, :], ACT.Copy)
                    ins = A(f_raw[:, :], b[32:32 + HEADS, :], ACT.Copy)
                elif mt == GQ:
                    ins = A(g_q[:, :], b[:, :], ACT.Copy, scale=DK ** -0.5)
                elif mt == GK:
                    ins = A(g_k[:, :], b[:, :], ACT.Copy)
                elif mt < TOK_A:
                    q = mt < FK
                    h = 2 * (mt - (FQ if q else FK))
                    for i in range(2):
                        ins = A((f_q if q else f_k)[0:DH, h + i, :], b[DH * i:DH * i + DH, :], ACT.Copy,
                                scale=DH ** -0.5 if q else 1.0)
                elif mt < MQ:
                    ins = A(values[:, mt - TOK_A, 0:512], b[:, :], ACT.Copy)
                elif mt < MK:
                    ins = A(m_q[:, mt - MQ, :], b[:, :], ACT.Copy, scale=DH ** -0.5)
                elif mt < TOK_B:
                    ins = A(m_k[:, mt - MK, :], b[:, :], ACT.Copy)
                elif mt < GATE:
                    t = mt - TOK_B
                    A(values[:, t, 512:768], b[:, 0:256], ACT.Copy)
                    ins = A(values[:, t, 768:1024], b[:, 256:512], ACT.Silu)
                else:
                    g = mt - GATE
                    if g >= GATE_SLOTS:
                        act_e.wait_ge(up_read, g - GATE_SLOTS + 1)
                    ins = A(gates[:, g % GATE_SLOTS, :], b[:, :], ACT.Copy if g < GATE_SLOTS else ACT.Sigmoid)
                ins.then_inc(proj_read, 1)

            def ratio_exp(n):
                act_e.wait_ge(diff_ready, n + 1)
                link(A(ratio[:, :], ratio[:, :], ACT.Abs))
                A(ratio[:, :], ratio[:, :], ACT.Exp, scale=-1.0 / TAU).then_inc(ratio_ready, 1)

            high(0)
            for h in range(4):
                act_e.wait_ge(x_in[h], 16)
                A(xT_hi[:, 2 * h:2 * h + 2, :], xT_in[:, 2 * h:2 * h + 2, :], ACT.Copy).then_inc(x_hi, 1)
            high(1)
            for kind, n in EARLY:
                if kind == "mt":
                    copy_out(n)
                elif kind == "tok" and n // TT % 2:
                    copy_out((TOK_A if n < 2 * TT else TOK_B) + n % TT)
                elif kind == "decay":
                    act_e.wait_ge(decay_pre, 1)
                    link(A(log1p[:, :], bank[4][:, :], ACT.Abs, bias=a_b_sb[:, 0:1]))
                    link(A(f_log[:, :], f_raw[:, :], ACT.Abs, bias=fb_sb[:, 0:1]))
                    link(A(log1p[:, :], log1p[:, :], ACT.Exp, scale=-1.0))
                    link(A(f_log[:, :], f_log[:, :], ACT.Exp, scale=-1.0))
                    A(log1p[:, :], log1p[:, :], ACT.Ln, bias=1.0)
                    A(f_log[:, :], f_log[:, :], ACT.Ln, bias=1.0).then_inc(log_ready, 1)
                    ratio_exp(0)
                    ratio_exp(1)
                elif kind == "level":
                    if n + 2 < 7:
                        ratio_exp(n + 2)
                    if n == 5:
                        act_e.wait_ge(level_read, 6)
                        act_e.wait_ge(qk_ready, 7)
                        A(end_dec[:, :], decay[:, P - 1::P], ACT.Exp, scale=-1.0 / TAU)
                        A(ratio[:, :], decay[:, :], ACT.Exp, scale=-1.0 / TAU).then_inc(ratio_ready, 1)
                    if n == 6:
                        act_e.wait_ge(diff_ready, 8)
                        A(k_end[:, :], k_end[:, :], ACT.Exp, scale=1.0 / TAU).then_inc(ratio_ready, 1)
                elif kind == "carry" and n == 0:
                    act_e.wait_ge(carry_pe, 1)
                    A(k_endT[:, :], bank[5][:, :], ACT.Copy).then_inc(carry_act, 1)
                elif kind == "carry" and n == 2:
                    act_e.wait_ge(carry_pe, 3)
                    for i in range(2):
                        A(squares[:, 512 * i:512 * i + 512], bank[4 + i][:, :], ACT.Square).then_inc(carry_act, 1)
                    act_e.wait_ge(carry_dve, 3)
                    A(rms[:, :], rms[:, :], ACT.Sqrt).then_inc(carry_act, 1)
                after(kind, n)

            def gate_sigmoid(d):
                act_e.wait_ge(proj_read, GATE + 3 * d + 3)
                A(gates[:, 3 * d:3 * d + 3, :], gates[:, 3 * d:3 * d + 3, :], ACT.Sigmoid).then_inc(gate_sig, 1)

            for s in range(FILL_STEPS + 1):
                if s == 1:
                    act_e.wait_ge(carry_pe, 4)
                    for i in range(2):
                        A(yT_hi[:, 2 + i, :], bank[6 + i][:, :], ACT.Copy).then_inc(yT_hi_ready, 1)
                if s < UNITS:
                    act_e.wait_ge(max_ready, s + 1)
                    if s >= 2:
                        act_e.wait_ge(pT_done, s - 1)
                    n = (unit(s)[2] + 1) * P
                    A(probs[s % 2][:, 0:n], bank[4 + s % 2][:, 0:n], ACT.Exp, bias=row_max[:, s % 2:s % 2 + 1],
                      accum_out=row_sum[:, s % 2:s % 2 + 1]).then_inc(exp_done, 1)
                if 1 <= s <= UNITS:
                    u = s - 1
                    act_e.wait_ge(pT_done, u + 1)
                    if u >= 2:
                        act_e.wait_ge(pv_done, u - 1)
                    n = (unit(u)[2] + 1) * P
                    A(probsT[u % 2][:, 0:n], bank[6][:, 0:n], ACT.Copy).then_inc(pT_read, 1)
                if s >= 10 and (s - 10) % 8 == 0:
                    pair = (s - 10) // 8
                    act_e.wait_ge(pv_done, 8 * pair + 8)
                    A(yT_hi[:, (0, 1, 4, 5)[pair], :], bank[7][:, :], ACT.Copy).then_inc(yT_hi_ready, 1)
                if s >= 3 and s % 3 == 0:
                    g = s // 3 - 1
                    copy_out(GATE + g)
                    after("gate", g)
                if s > UNITS:
                    gate_sigmoid(s - UNITS - 1)
            for kind, n in LATE:
                if kind == "gate":
                    copy_out(GATE + n)
                else:
                    act_e.wait_ge(merged_ready, n + 1)
                    A(merged_hi[:, n, :], mix_acc[n % 2][:, :], ACT.Copy).then_inc(merged_hi_ready, 1)
                after(kind, n)
            for n in range(2):
                after("out", n)
            def expert_high(w, e, p, m):
                w.wait_raw(act_e, e, p, m)
                A(w_hi[m % 4][:, :], w.raw(p, m)[:, :], ACT.Copy).then_inc(w.hi, 1)

            act_e.wait_ge(used, N_MIX - 1)
            expert_high(first, 0, 0, 0)
            for t in range(TT):
                act_e.wait_ge(var_ready, t + 1)
                A(std[:, t:t + 1], std[:, t:t + 1], ACT.Sqrt).then_inc(std_ready, 1)
                act_e.wait_ge(shift_ready, t + 1)
                A(x1[:, t, :], x1[:, t, :], ACT.Identity, bias=shift[:, t:t + 1], scale=std[:, t:t + 1]).then_inc(normed, 1)
            for n in range(2 * TT):
                act_e.wait_ge(x1T_done, n + 1)
                t, h = n // 2, n % 2
                A(x1T[:, 4 * h:4 * h + 4, t * P:(t + 1) * P], bank[n % 4][:, :].rearrange("p (k n) -> p k n", k=4),
                  ACT.Copy).then_inc(x1T_read, 1)
                if n == 3:
                    act_e.wait_ge(used, N_MIX)
                    expert_high(first, 0, 0, 1)
            act_e.wait_ge(x1_out, 16 * TT)
            expert_high(first, 0, 0, 2)
            act_e.wait_ge(logit_done, 2)
            expert_high(first, 0, 0, 3)
            act_e.wait_ge(top_ready, 1)
            A(exp4[:, :, :], exp4[:, :, :], ACT.Exp).then_inc(gate_exp, 1)
            def xe_high(w, h, src):
                A(xe_hi[:, 4 * h:4 * h + 4, :], src[:, :].rearrange("p (k n) -> p k n", k=4), ACT.Copy)\
                    .then_inc(w.tr_hi, 1)

            def expert(w, e, p, last_one):
                n_a, n_b = w.transposes(e, last_one)
                pipelined = not w.alone and not last_one
                if w.alone:
                    for m in range(SPLIT):
                        expert_high(w, e, p, m)
                    for h in range(2):
                        act_e.wait_ge(w.tr, e * 4 + (h + 1))
                        xe_high(w, h, bank[6 + h])
                for m in range(CPE):
                    if m == 6:
                        act_e.wait_ge(w.tr, n_a + 1)
                        A(aT_hi[0][:, :, :], bank[6][:, :].rearrange("p (k n) -> p k n", k=4), ACT.Copy).then_inc(w.tr_hi, 1)
                    if m == 7:
                        act_e.wait_ge(w.glu_read, e * 2 + 2)
                        A(glu_s[:, :], glu_g[:, :], ACT.Sigmoid, scale=SWIGLU).then_inc(w.sig, 1)
                        if pipelined:
                            act_e.wait_ge(w.tr, n_a + 2)
                            xe_high(w, 0, bank[7])
                    act_e.wait_ge(w.used, e * CPE + (m + 1))
                    if m == 9:
                        act_e.wait_ge(w.tr, n_b + 1)
                        A(aT_hi[1][:, :, :], (bank[6] if pipelined else bank[7])[:, :].rearrange("p (k n) -> p k n", k=4),
                          ACT.Copy).then_inc(w.tr_hi, 1)
                        if pipelined:
                            act_e.wait_ge(w.tr, n_b + 2)
                            xe_high(w, 1, bank[7])
                    if m == 11:
                        if not w.alone and not (isinstance(e, int) and e == 0):
                            act_e.wait_ge(w.scattered, e * 16)
                        for b in range(2):
                            ins = A(y_sb[:, 512 * b:512 * b + 512], bank[4 + b][:, :], ACT.Copy)
                        ins.then_inc(w.y_copied, 1)
                    if m + LOOK < CPE or pipelined:
                        expert_high(w, e, p, m + LOOK)
                    if m == 3:
                        act_e.wait_ge(w.glu_read, e * 2 + 1)
                        A(glu_s[:, :], glu_g[:, :], ACT.Sigmoid, scale=SWIGLU).then_inc(w.sig, 1)

            for h in range(2):
                act_e.wait_ge(first.tr, h + 1)
                xe_high(first, h, bank[6 + h])
            passes(act_e, lambda e, p, last_one: expert(first, e, p, last_one))
            n = act_e.value_load(n_extra[0:1, 0:1], min_val=0, max_val=MAX_EXTRA)
            with act_e.If(n > 0):
                with act_e.Fori(0, MAX_EXTRA) as j:
                    with act_e.If(j < n):
                        expert(more, j, 0, False)
                    act_e.nop()
            act_e.nop()
            act_e.wait_ge(x_end_in, 16)
            A(x_end[:, :, :], x_end[:, :, :], ACT.Copy, scale=ALPHA).then_inc(x_scaled, 1)

            def scale_last(t):
                act_e.wait_ge(y_in[t], 16)
                A(res[t][:, :], y_rows[t][:, PE_ROWS, :], ACT.Copy, scale=gate_w[:, t, PE_ROWS:TOPK]).then_inc(last_row, 1)

            scale_last(0)
            for t in range(TT):
                if t + 1 < TT:
                    scale_last(t + 1)
                act_e.wait_ge(end_var, t + 1)
                A(std[:, t:t + 1], std[:, t:t + 1], ACT.Sqrt).then_inc(end_std, 1)
                act_e.wait_ge(end_shift, t + 1)
                A(ln_t[t][:, :], res[t][:, :], ACT.Identity, bias=shift[:, t:t + 1], scale=std[:, t:t + 1]).then_inc(end_normed, 1)

        @block.vector
        def _(dve):
            link = linked(dve, dve_step)
            TTO, TS, STT = dve.tensor_tensor, dve.tensor_scalar, dve.scalar_tensor_tensor

            def low(c):
                dve.wait_ge(m_hi, c + 1)
                if c - 1 in POOL_MIX:
                    dve.wait_ge(m_lo, c)
                n = D if c == 0 else CW
                TTO(w_lo[c % 2][:, 0:n], raw[c % RAW_MIX][:, 0:n], w_hi[c % 2][:, 0:n].bitcast(F32), ALU.subtract)\
                    .then_inc(m_lo, 1)

            def after(kind, n):
                c = freed(kind, n)
                if c is not None and c + 2 < N_MIX and c + 2 not in POOL_MIX:
                    low(c + 2)

            def blocks(x, size):
                return x[:, :].rearrange("p (n s) -> p n s", s=size)

            def difference(n):
                s = 2 * LEVELS[n]
                if n >= 1:
                    dve.wait_ge(qk_ready, n)
                ref = blocks(decay, s)[:, :, LEVELS[n] - 1:LEVELS[n]].to_broadcast([P, T // s, s])
                TTO(blocks(ratio, s), blocks(decay, s), ref, ALU.subtract).then_inc(diff_ready, 1)

            def scale_qk(n):
                dve.wait_ge(ratio_ready, n + 1)
                if n >= 2:
                    dve.wait_ge(level_done, n - 1)
                TTO(q_dec[n % 2][:, :], g_q[:, :], ratio[:, :], ALU.mult)
                TTO(k_dec[n % 2][:, :], g_k[:, :], ratio[:, :], ALU.mult).then_inc(qk_ready, 1)

            low(0)
            for h in range(4):
                dve.wait_ge(x_hi, h + 1)
                TTO(xT_lo[:, 2 * h:2 * h + 2, :], xT_in[:, 2 * h:2 * h + 2, :], xT_hi[:, 2 * h:2 * h + 2, :].bitcast(F32),
                    ALU.subtract).then_inc(x_lo, 1)
            low(1)
            for kind, n in EARLY:
                if kind == "decay":
                    dve.wait_ge(log_ready, 1)
                    dve.wait_ge(cst_in, 32)
                    link(TS(ratio[:, :], bank[4][:, :], a_b_sb[:, 0:1], 0.0, ALU.add, ALU.min))
                    link(TS(f_raw[:, :], f_raw[:, :], fb_sb[:, 0:1], 0.0, ALU.add, ALU.min))
                    link(TTO(ratio[:, :], log1p[:, :], ratio[:, :], ALU.subtract))
                    link(TTO(f_log[:, :], f_log[:, :], f_raw[:, :], ALU.subtract))
                    for t in range(TT):
                        dve.tensor_tensor_scan(decay[:, t * P:(t + 1) * P], ones, ratio[:, t * P:(t + 1) * P], 0.0,
                                               ALU.mult, ALU.add)
                        link(dve.tensor_tensor_scan(f_cum[:, t * P:(t + 1) * P], ones[0:HEADS, :], f_log[:, t * P:(t + 1) * P],
                                                    f_cum[:, t * P - 1:t * P] if t else 0.0, ALU.mult, ALU.add))
                    dve.tensor_copy(f_raw[:, :], f_cum[:, :]).then_inc(crow_ready, 1)
                    dve.wait_ge(proj_read, 3)
                    for m in range(2):
                        difference(m)
                        scale_qk(m)
                elif kind == "level":
                    dve.wait_ge(level_done, n + 1)
                    if n == 0:
                        dve.wait_ge(gla_in, 96)
                        dve.wait_ge(pool_ready, 1)
                    mask = level_mask[:, n, :].unsqueeze(1).to_broadcast([P, TT, P])
                    for h in range(HEADS):
                        ins = dve.copy_predicated(scoreT[:, h, :].rearrange("p (t s) -> p t s", t=TT), mask,
                                                  bank[4 + h][:, :].rearrange("p (t s) -> p t s", t=TT))
                    ins.then_inc(level_read, 1)
                    if n + 2 < 7:
                        difference(n + 2)
                        scale_qk(n + 2)
                    if n == 4:
                        b = blocks(decay, P)
                        TTO(blocks(k_end, P), b, b[:, :, P - 1:P].to_broadcast([P, TT, P]), ALU.subtract).then_inc(diff_ready, 1)
                    if n == 6:
                        dve.wait_ge(ratio_ready, 8)
                        TTO(q_dec[1][:, :], g_q[:, :], ratio[:, :], ALU.mult)
                        dve.wait_ge(ratio_ready, 9)
                        TTO(k_end[:, :], g_k[:, :], k_end[:, :], ALU.mult).then_inc(carry_dve, 1)
                elif kind == "carry" and n == 1:
                    dve.wait_ge(carry_pe, 2)
                    for t in range(3):
                        link(TTO(state[:, t, :], bank[6 + t // 2][:, (t % 2) * 256:(t % 2) * 256 + 256], head_mask[:, :], ALU.mult))
                    link(STT(state[:, 1, :], state[:, 0, :], end_dec[:, 1:2], state[:, 1, :], ALU.mult, ALU.add))
                    STT(state[:, 2, :], state[:, 1, :], end_dec[:, 2:3], state[:, 2, :], ALU.mult, ALU.add).then_inc(carry_dve, 1)
                elif kind == "carry" and n == 2:
                    dve.wait_ge(carry_act, 3)
                    link(dve.tensor_reduce(rms[:, :], squares[:, :].rearrange("p (g d) -> p g d", d=DH), AX.X, ALU.add))
                    TS(rms[:, :], rms[:, :], 1.0 / DH, RMS_EPS, ALU.mult, ALU.add).then_inc(carry_dve, 1)
                    dve.wait_ge(carry_act, 4)
                    dve.wait_ge(crow_in, 16 * HEADS)
                    link(dve.reciprocal(rms[:, :], rms[:, :]))
                    for i in range(2):
                        yv = y_gla[:, 2 * i:2 * i + 2, :].rearrange("p t (h d) -> p (t h) d", d=DH)
                        ins = TTO(yv, bank[4 + i][:, :].rearrange("p (g d) -> p g d", d=DH),
                                  rms[:, 8 * i:8 * i + 8].unsqueeze(2).to_broadcast([P, 8, DH]), ALU.mult)
                    ins.then_inc(y_scaled, 1)
                    dve.wait_ge(y_scaled, 1)
                    TTO(y_gla[:, :, :], y_gla[:, :, :], norm_gb[:, :].unsqueeze(1).to_broadcast([P, TT, 256]), ALU.mult)\
                        .then_inc(y_scaled, 1)
                after(kind, n)

            for s in range(FILL_STEPS + 1):
                if s == 0:
                    dve.wait_ge(proj_read, GATE)
                    dve.wait_ge(y_scaled, 2)
                    TTO(y_gla[:, :, :], y_gla[:, :, :], values[:, :, 768:1024], ALU.mult).then_inc(carry_dve, 1)
                if s == 1:
                    for i in range(2):
                        dve.wait_ge(yT_hi_ready, i + 1)
                        TTO(yT_lo[:, 2 + i, :], bank[6 + i][:, :], yT_hi[:, 2 + i, :].bitcast(F32), ALU.subtract)\
                            .then_inc(yT_lo_ready, 1)
                if s < UNITS:
                    dve.wait_ge(score_done, s + 1)
                    n = (unit(s)[2] + 1) * P
                    m = slice(s % 2, s % 2 + 1)
                    dve.tensor_reduce(row_max[:, m], bank[4 + s % 2][:, 0:n], AX.X, ALU.max, negate=True).then_inc(max_ready, 1)
                    dve.wait_ge(exp_done, s + 1)
                    link(dve.reciprocal(row_inv[:, m], row_sum[:, m]))
                    TS(probs[s % 2][:, 0:n], probs[s % 2][:, 0:n], row_inv[:, m], None, ALU.mult).then_inc(norm_done, 1)
                if s >= 10 and (s - 10) % 8 == 0:
                    pair = (s - 10) // 8
                    dve.wait_ge(yT_hi_ready, 3 + pair)
                    y = (0, 1, 4, 5)[pair]
                    TTO(yT_lo[:, y, :], bank[7][:, :], yT_hi[:, y, :].bitcast(F32), ALU.subtract).then_inc(yT_lo_ready, 1)
                if s >= 3 and s % 3 == 0:
                    after("gate", s // 3 - 1)

            for kind, n in LATE:
                if kind == "up":
                    if n < 4:
                        dve.wait_ge(gate_sig, n + 1)
                    else:
                        dve.wait_ge(proj_read, GATE + 3 * n + 3)
                    if n >= 2:
                        dve.wait_ge(merged_hi_ready, n - 1)
                    acc, tmp = mix_acc[n % 2], mix_tmp
                    for b in range(3):
                        i = 3 * n + b
                        dve.wait_ge(*up_signal(i))
                        to = acc if b == 0 else tmp[b - 1]
                        TTO(to[:, :], bank[4 + i % 4][:, :], gates[:, i % GATE_SLOTS, :], ALU.mult).then_inc(up_read, 1)
                    dve.wait_ge(up_read, 3 * n + 3)
                    link(TTO(acc[:, :], acc[:, :], tmp[0][:, :], ALU.add))
                    TTO(acc[:, :], acc[:, :], tmp[1][:, :], ALU.add).then_inc(merged_ready, 1)
                    dve.wait_ge(merged_hi_ready, n + 1)
                    TTO(merged_lo[:, n, :], acc[:, :], merged_hi[:, n, :].bitcast(F32), ALU.subtract).then_inc(merged_lo_ready, 1)
                after(kind, n)
            for n in range(2):
                after("out", n)

            dve.wait_ge(tok_in, 64)

            def residual(half, t):
                cols = slice(512 * half, 512 * half + 512)
                link(STT(x1[:, t, cols], x_tok[:, t, cols], ALPHA, bank[4 * half + t][:, :], ALU.mult, ALU.add))
                link(dve.bn_stats(stats[:, t, 6 * half:6 * half + 6], x1[:, t, cols]))

            def shift_of(t):
                dve.wait_ge(std_ready, t + 1)
                link(dve.reciprocal(std[:, t:t + 1], std[:, t:t + 1]))
                STT(shift[:, t:t + 1], mean_var[:, t, 0:1], -1.0, std[:, t:t + 1], ALU.mult, ALU.mult).then_inc(shift_ready, 1)

            def norm_weight(t):
                dve.wait_ge(normed, t + 1)
                TTO(x1[:, t, :], x1[:, t, :], ln_g[:, :], ALU.mult).then_inc(scaled, 1)

            def expert_low(w, e, p, m):
                dve.wait_ge(w.hi, e * CPE + (m + 1))
                TTO(w_lo[m % 4][:, :], w.raw(p, m)[:, :], w_hi[m % 4][:, :].bitcast(F32), ALU.subtract).then_inc(w.lo_dve, 1)

            dve.wait_ge(used, N_MIX - 2)
            for t in range(TT):
                residual(0, t)
            for t in range(TT + 1):
                if t < TT:
                    dve.wait_ge(*((out_tile, 3 * TT + t - 2) if t < TT - 1 else (used, N_MIX)))
                    residual(1, t)
                    link(dve.bn_aggr(mean_var[:, t, :], stats[:, t, :]))
                    TS(std[:, t:t + 1], mean_var[:, t, 1:2], LN_EPS, None, ALU.add).then_inc(var_ready, 1)
                    shift_of(t)
                if t:
                    norm_weight(t - 1)
            dve.wait_ge(scaled, TT)
            dve.wait_ge(x1_ready, TT - 1)
            TTO(x1[:, TT - 1, :], x1[:, TT - 1, :], ln_b[:, :], ALU.add).then_inc(x1_ready, 1)
            for m in range(2):
                expert_low(first, 0, 0, m)
            dve.wait_ge(bias_split, 1)
            dve.wait_ge(used, N_MIX)
            dve.tensor_copy(bias3[:, :], bias_parts[:, :]).then_inc(bias_ready, 1)
            for i, tiles in enumerate((slice(0, TT - 1), slice(TT - 1, TT))):
                dve.wait_ge(logit_done, i + 1)
                n = tiles.stop - tiles.start
                link(TTO(logits[:, tiles, :], bank[4 + 3 * i][:, 0:TT * E].rearrange("p (t e) -> p t e", t=TT)[:, tiles, :],
                         b_r[:, :].unsqueeze(1).to_broadcast([P, n, E]), ALU.add))
                for t in range(tiles.start, tiles.stop):
                    link(dve.max(top_v[:, t, :], logits[:, t, :]))
                for t in range(tiles.start, tiles.stop):
                    link(dve.max_index(top_i[:, t, :], top_v[:, t, :], logits[:, t, :]))
            TTO(exp4[:, :, :], top_v[:, :, 0:TOPK], top_v[:, :, 0:1].to_broadcast([P, TT, TOPK]), ALU.subtract)\
                .then_inc(top_ready, 1)
            link(dve.tensor_copy(ix_f[:, :, :], top_i[:, :, 0:TOPK]))
            link(TTO(chosen[:, :, :, :], iota[:, 0:E].unsqueeze(1).unsqueeze(1).to_broadcast([P, TT, TOPK, E]),
                     ix_f[:, :, :].unsqueeze(3).to_broadcast([P, TT, TOPK, E]), ALU.is_equal))
            with nc.allow_low_precision(reason="sums of zeros and at most one one"):
                dve.tensor_reduce(hits[:, :, :], chosen[:, :, :, :].rearrange("p t k e -> p t e k"), AX.X, ALU.add)\
                   .then_inc(hits_ready, 1)
            rows = row_id.rearrange("p (k t) -> p t k", t=TT).unsqueeze(3).to_broadcast([P, TT, TOPK, E])
            TTO(row_of[:, :, :, :], chosen[:, :, :, :], rows, ALU.mult)
            dve.wait_ge(pos_done, 1)
            link(TTO(places_of[:, :, :, :], chosen[:, :, :, :],
                     bank[5][:, 0:TT * E].rearrange("p (t e) -> p t e", t=TT).unsqueeze(2).to_broadcast([P, TT, TOPK, E]),
                     ALU.mult))
            link(dve.tensor_reduce(pos[:, :], places_of[:, :, :, :].rearrange("p t k e -> p (t k) e"), AX.X, ALU.add))
            link(TS(blk[:, :], pos[:, :], float(P), None, ALU.is_ge))
            for b in (2, 3):
                link(STT(blk[:, :], pos[:, :], float(b * P), blk[:, :], ALU.is_ge, ALU.add))
            STT(slot[:, :], blk[:, :], -float(P), pos[:, :], ALU.mult, ALU.add).then_inc(slot_ready, 1)
            TTO(blk_is[:, :, :], iota[:, 0:NB].unsqueeze(1).to_broadcast([P, TT * TOPK, NB]),
                blk[:, :].unsqueeze(2).to_broadcast([P, TT * TOPK, NB]), ALU.is_equal).then_inc(slot_ready, 1)
            dve.wait_ge(slot_ready, 2)
            for i in range(2):
                n = slice(i * HALF, i * HALF + HALF)
                shape = [P, HALF, P]
                ins = TTO(onehot_s[:, n, :], iota.unsqueeze(1).to_broadcast(shape), slot[:, n].unsqueeze(2).to_broadcast(shape),
                          ALU.is_equal)
                if i == 0:
                    ins = block_rows(dve, 0)
                ins.then_inc(onehot_ready, 1)
            dve.wait_ge(gate_exp, 1)
            link(dve.tensor_reduce(exp_sum[:, :], exp4[:, :, :], AX.X, ALU.add))
            link(dve.reciprocal(exp_sum[:, :], exp_sum[:, :]))
            link(TTO(gate_w[:, :, :], exp4[:, :, :], exp_sum[:, :].unsqueeze(2).to_broadcast([P, TT, TOPK]), ALU.mult))
            dve.wait_ge(onehot_used, 1)
            link(TS(table[:, :], bank[6][:, 0:P], -1.0, None, ALU.add))
            dve.tensor_copy(scatter_ix[:, :], table[:, :])
            link(TS(wrap[:, :], table[:, :], float(T), None, ALU.is_ge))
            for k in (2, 3):
                link(STT(wrap[:, :], table[:, :], float(k * T), wrap[:, :], ALU.is_ge, ALU.add))
            link(STT(wrapped[:, :], wrap[:, :], -float(T), table[:, :], ALU.mult, ALU.add))
            dve.tensor_copy(gather_ix[:, :], wrapped[:, :]).then_inc(route_ready, 1)
            dve.wait_ge(counted, 1)
            link(dve.tensor_copy(counts[:, :], bank[7][0:1, 0:E]))
            link(TS(over[:, :], counts[:, :], float(P), None, ALU.is_gt))
            for k in (2, 3):
                link(STT(over[:, :], counts[:, :], float(k * P), over[:, :], ALU.is_gt, ALU.add))
            link(dve.tensor_reduce(junk[0:1, 0:1], over[:, :], AX.X, ALU.add))
            dve.tensor_copy(n_extra[:, :], junk[0:1, 0:1]).then_inc(route_ready, 1)
            def xe_low(w, h, src):
                TTO(xe_lo[:, 4 * h:4 * h + 4, :], src[:, :].rearrange("p (k n) -> p k n", k=4),
                    xe_hi[:, 4 * h:4 * h + 4, :].bitcast(F32), ALU.subtract).then_inc(w.tr_lo, 1)

            def act_low(w, h, src):
                TTO(aT_lo[h][:, :, :], src[:, :].rearrange("p (k n) -> p k n", k=4), aT_hi[h][:, :, :].bitcast(F32),
                    ALU.subtract).then_inc(w.tr_lo, 1)

            def clamp(w, e, half):
                dve.wait_ge(w.used, e * CPE + (4 * half + 4))
                TS(glu_g[:, :], bank[2 * half][:, :], LIMIT, None, ALU.min)
                TS(glu_u[:, :], bank[2 * half + 1][:, :], LIMIT, -LIMIT, ALU.min, ALU.max).then_inc(w.glu_read, 1)

            def activate(w, e, half):
                dve.wait_ge(w.sig, e * 2 + (half + 1))
                TTO(glu_g[:, :], glu_g[:, :], glu_s[:, :], ALU.mult).then_inc(w.gated, 1)
                dve.wait_ge(w.gated, e * 2 + (half + 1))
                STT(act[half][:, :], glu_u[:, :], 1.0, glu_g[:, :], ALU.add, ALU.mult).then_inc(w.act_ready, 1)

            def expert(w, e, p, last_one):
                n_a, n_b = w.transposes(e, last_one)
                pipelined = not w.alone and not last_one
                if w.alone:
                    for m in range(SPLIT):
                        expert_low(w, e, p, m)
                    for h in range(2):
                        dve.wait_ge(w.tr_hi, e * 4 + (h + 1))
                        xe_low(w, h, bank[6 + h])
                for m in range(CPE):
                    if m == 3:
                        clamp(w, e, 0)
                    if m == 6:
                        dve.wait_ge(w.tr_hi, n_a + 1)
                        act_low(w, 0, bank[6])
                    if m == 7:
                        clamp(w, e, 1)
                        if pipelined:
                            dve.wait_ge(w.tr_hi, n_a + 2)
                            xe_low(w, 0, bank[7])
                        activate(w, e, 1)
                    if m == 8:
                        dve.wait_ge(w.tr_hi, n_b + 1)
                        act_low(w, 1, bank[6] if pipelined else bank[7])
                        if pipelined:
                            dve.wait_ge(w.tr_hi, n_b + 2)
                            xe_low(w, 1, bank[7])
                    if (m + LOOK < CPE or pipelined) and (m + LOOK) % CPE in w.dve_chunks:
                        expert_low(w, e, p, m + LOOK)
                    if m == 3:
                        activate(w, e, 0)

            dve.wait_ge(first.lo_dve, SPLIT)
            for h in range(2):
                dve.wait_ge(first.tr_hi, h + 1)
                xe_low(first, h, bank[6 + h])
            passes(dve, lambda e, p, last_one: expert(first, e, p, last_one))
            n = dve.value_load(n_extra[0:1, 0:1], min_val=0, max_val=MAX_EXTRA)
            elinks = linked(dve, end_step)
            with dve.If(n > 0):
                elink = linked(dve, extra_step)
                dve.wait_ge(extra_in, 16)
                elink(TTO(extra_on[:, :].rearrange("p (e b) -> p e b", b=NB), counts[:, :].unsqueeze(2).to_broadcast([1, E, NB]),
                          extra_cst[:, 0:P].rearrange("p (e b) -> p e b", b=NB), ALU.is_gt))
                elink(dve.tensor_tensor_scan(extra_sum[:, :], ones[0:1, :], extra_on[:, :], 0.0, ALU.mult, ALU.add))
                elink(TTO(extra_on[:, :], extra_on[:, :], iota[0:1, :], ALU.mult))
                elink(TTO(extra_eq[:, :, :], extra_sum[:, :].unsqueeze(1).to_broadcast([1, 16, P]),
                          extra_cst[:, P:P + 16].unsqueeze(2).to_broadcast([1, 16, P]), ALU.is_equal))
                elink(TTO(extra_eq[:, :, :], extra_eq[:, :, :], extra_on[:, :].unsqueeze(1).to_broadcast([1, 16, P]), ALU.mult))
                elink(dve.tensor_reduce(extra_f[:, :], extra_eq[:, :, :], AX.X, ALU.add))
                dve.tensor_copy(extra[:, :], extra_f[:, :]).then_inc(extra_ready, 1)
                with dve.Fori(0, MAX_EXTRA) as j:
                    with dve.If(j < n):
                        expert(more, j, 0, False)
                    dve.nop()
            dve.nop()
            dve.wait_ge(ln2_in, 32)
            for t in range(TT + 1):
                if t < TT:
                    r = res[t]
                    dve.wait_ge(with_x, t + 1)
                    for h in range(2):
                        cols = slice(512 * h, 512 * h + 512)
                        dve.wait_ge(end_first, 2 * t + h + 1)
                        elinks(TTO(r[:, cols], r[:, cols], bank[2 * t + h][:, :], ALU.add))
                        elinks(dve.bn_stats(stats[:, t, 6 * h:6 * h + 6], r[:, cols]))
                    elinks(dve.bn_aggr(mean_var[:, t, :], stats[:, t, :]))
                    TS(std[:, t:t + 1], mean_var[:, t, 1:2], LN_EPS, None, ALU.add).then_inc(end_var, 1)
                    dve.wait_ge(end_std, t + 1)
                    elinks(dve.reciprocal(std[:, t:t + 1], std[:, t:t + 1]))
                    STT(shift[:, t:t + 1], mean_var[:, t, 0:1], -1.0, std[:, t:t + 1], ALU.mult, ALU.mult).then_inc(end_shift, 1)
                if t:
                    dve.wait_ge(end_normed, t)
                    TTO(ln_t[t - 1][:, :], ln_t[t - 1][:, :], ln2g[:, :], ALU.mult).then_inc(end_scaled, 1)
            dve.wait_ge(end_scaled, TT)
            TTO(ln_t[TT - 1][:, :], ln_t[TT - 1][:, :], ln2b[:, :], ALU.add).then_inc(last_ready, 1)

        @block.gpsimd
        def _(pool):
            pool.memset(scoreT[:, :, :], 0.0)
            pool.wait_ge(cst_in, 32)
            pool.tensor_copy(cst_b[:, :], cst_b_in[:, :])
            pool.wait_ge(gla_in, 96)
            pool.tensor_copy(level_mask[:, :, :], mask_in[:, :, :]).then_inc(pool_ready, 1)
            pool.wait_ge(pool_ready, 1)
            pool.memset(f_q[DH:DH + 1, :, :], 1.0).then_inc(pool_ready, 1)
            pool.wait_ge(pool_ready, 2)
            pool.memset(pool_idle[:, :], 0.0).then_inc(pool_ready, 1)
            pool.wait_ge(pool_ready, 3)
            pool.wait_ge(crow_ready, 1)
            for h in range(HEADS):
                pool.dma_start(f_k[DH:DH + 1, h, :], f_raw[h:h + 1, :]).then_inc(crow_in, 16)
            for c in POOL_MIX:
                pool.wait_ge(m_hi, c + 1)
                pool.wait_ge(m_lo, c)
                pool.tensor_tensor(w_lo[c % 2][:, :], raw[c % RAW_MIX][:, :], w_hi[c % 2][:, :].bitcast(F32), ALU.subtract)\
                    .then_inc(m_lo, 1)
            pool.wait_ge(bias_in, 48)
            step = linked(pool, bias_step)
            step(pool.tensor_copy(bias_parts[:, :], bias_f[:, :]))
            step(pool.tensor_tensor(bias_f[:, :], bias_f[:, :], bias_parts[:, :], ALU.subtract))
            step(pool.tensor_copy(bias_parts[32:64, :], bias_f[32:64, :]))
            step(pool.tensor_copy(bias_parts[64:96, :], bias_f[64:96, :]))
            step(pool.tensor_tensor(bias_f[64:96, :], bias_f[64:96, :], bias_parts[64:96, :], ALU.subtract))
            pool.tensor_copy(bias_parts[64:96, :], bias_f[64:96, :]).then_inc(bias_split, 1)
            pool.wait_ge(bias_split, 1)
            for t in range(TT - 1):
                pool.wait_ge(scaled, t + 1)
                pool.tensor_tensor(x1[:, t, :], x1[:, t, :], ln_b[:, :], ALU.add).then_inc(x1_ready, 1)
            pool.wait_ge(used, N_MIX)
            pool.memset(x_rows[:, :], 0.0).then_inc(pool_ready, 1)
            for m in (2, 3):
                pool.wait_ge(first.hi, m + 1)
                pool.wait_ge(first.lo_dve, m)
                pool.tensor_tensor(w_lo[m][:, :], raw[m][:, :], w_hi[m][:, :].bitcast(F32), ALU.subtract)\
                    .then_inc(first.lo_dve, 1)
            pool.wait_ge(slot_ready, 2)
            block_rows(pool, 1).then_inc(rows_ready, 1)
            pool.wait_ge(pool_ready, 4)
            pool.wait_ge(x1_out, 16 * TT)
            pool.wait_ge(route_ready, 1)

            def gather(w, n, col):
                pool.tensor_copy(gix_now[:, :], gather_ix[:, bass.ds(col, 1)]).then_inc(w.gix, 1)
                pool.wait_ge(w.gix, n)
                pool.tensor_tensor(pool_idle[:, :], pool_idle[:, :], pool_idle[:, :], ALU.add)
                pool.indirect_dma_start(x_rows[:, :], None, x1_dram, bass.IndirectOffsetOnAxis(ap=gix_now[:, 0:1], axis=0),
                                        bounds_check=T - 1, oob_is_err=False).then_inc(w.gathered, 16)

            def scatter(w, n, col):
                pool.tensor_copy(six_now[:, :], scatter_ix[:, bass.ds(col, 1)]).then_inc(w.six, 1)
                pool.wait_ge(w.six, n)
                pool.tensor_tensor(pool_idle[:, :], pool_idle[:, :], pool_idle[:, :], ALU.add)
                pool.indirect_dma_start(y_dram, bass.IndirectOffsetOnAxis(ap=six_now[:, 0:1], axis=0), y_sb[:, :], None,
                                        bounds_check=TOPK * T - 1, oob_is_err=False).then_inc(w.scattered, 16)

            def expert_low(w, e, p, m):
                pool.wait_ge(w.hi, e * CPE + (m + 1))
                pool.tensor_tensor(w_lo[m % 4][:, :], w.raw(p, m)[:, :], w_hi[m % 4][:, :].bitcast(F32), ALU.subtract)\
                    .then_inc(w.lo_pool, 1)

            def expert(e, p, last_one):
                if not last_one:
                    pool.wait_ge(first.tr, e * 4 + 2)
                    gather(first, e + 2, (e + 1) * NB)
                if not (isinstance(e, int) and e == 0):
                    pool.wait_ge(first.y_copied, e)
                    scatter(first, e, (e - 1) * NB)
                for m in POOL_CHUNKS:
                    expert_low(first, e, p, m)

            gather(first, 1, 0)
            passes(pool, expert)
            pool.wait_ge(first.y_copied, E)
            scatter(first, E, (E - 1) * NB)
            first.wait_lo(pool, E - 1, CPE - 1)
            shape = [P, TT, PE_ROWS, P]
            pool.tensor_tensor(gate_diag[:, :, :, :], ident.unsqueeze(1).unsqueeze(1).to_broadcast(shape),
                               gate_w[:, :, 0:PE_ROWS].unsqueeze(3).to_broadcast(shape), ALU.mult).then_inc(diag_ready, 1)
            pool.wait_ge(first.scattered, 16 * E)
            n = pool.value_load(n_extra[0:1, 0:1], min_val=0, max_val=MAX_EXTRA)
            with pool.If(n > 0):
                with pool.Fori(0, MAX_EXTRA) as j:
                    with pool.If(j < n):
                        pool.wait_ge(extra_ready, 1)
                        col = pool.value_load(extra[0:1, bass.ds(j, 1)], min_val=0, max_val=P - 1)
                        gather(more, j + 1, col)
                        pool.wait_ge(more.y_copied, j + 1)
                        scatter(more, j + 1, col)
                        pool.wait_ge(more.scattered, (j + 1) * 16)
                        pool.nop()
                    pool.nop()
            pool.memset(gix_now[:, :], 0).then_inc(experts_done, 1)
            pool.wait_ge(ln2_in, 32)
            pool.wait_ge(x_scaled, 1)
            for t in range(TT + 1):
                if t < TT:
                    pool.wait_ge(last_row, t + 1)
                    pool.tensor_tensor(res[t][:, :], res[t][:, :], x_end[:, t, :], ALU.add).then_inc(with_x, 1)
                if t >= 2:
                    pool.wait_ge(end_scaled, t - 1)
                    pool.tensor_tensor(ln_t[t - 2][:, :], ln_t[t - 2][:, :], ln2b[:, :], ALU.add).then_inc(end_ready, 1)


def constants():
    import numpy as np

    r = np.arange(P)
    s, t = r[:, None], r[None, :]
    cf = np.zeros((P, 5 * P + 16), np.float32)
    cf[:, 0:P] = s == t
    cf[:, P:2 * P] = t
    cf[:, 2 * P:3 * P] = 1
    cf[:, 3 * P:3 * P + 16] = (np.arange(TOPK)[:, None] * T + np.arange(TT)[None, :] * P).reshape(1, 16) + s + 1
    cf[:, 3 * P + 16:] = (s // DK) == (np.arange(256)[None, :] // DH)
    cb = np.zeros((P, 4 * P + E), np.float32)
    cb[:, 0:P] = s == t
    cb[:, P:2 * P] = np.where(t <= s, 0.0, NEG)
    cb[:, 2 * P:3 * P] = s < t
    cb[:, 3 * P:4 * P] = 1
    cb[:96, 4 * P:] = (s[:96] % 32) == np.arange(E)[None, :]
    masks = np.zeros((P, 8, P), np.float32)
    for i, h in enumerate(LEVELS):
        masks[:, i, :] = (s // (2 * h) == t // (2 * h)) & (s % (2 * h) < h) & (t % (2 * h) >= h)
    masks[:, 7, :] = s == t
    extra = np.zeros((1, P + 16), np.float32)
    extra[0, :P] = np.where(r % NB, r % NB * P, 10 * T)
    extra[0, P:] = np.arange(16) + 1
    return cf, cb, masks, extra


def kernel(x, w_in, fox_fb, gla_a_up, gla_a_b, gla_norm_g, w_branch, w_out, ln1_g, ln1_b, w_router, b_router, w_gu, b_gu,
           w_dn, b_dn, ln2_g, ln2_b):
    import numpy as np
    import concourse.bacc as bacc
    from concourse.bass_utils import run_bass_kernel_spmd

    f32 = np.float32
    x, w_in, w_branch, w_out = (np.asarray(a)[0] for a in (x, w_in, w_branch, w_out))
    sizes = (256, 256, 256, 4, 128, 128, 256, 16, 256, 256, 256, 256, 3 * D)
    at = np.concatenate([[0], np.cumsum(sizes)])
    fq, fk, fv, ff, gq, gk, gv, ga, gr, mq, mk, mv, gt = (w_in[:, at[i]:at[i + 1]] for i in range(13))

    def by_tile(w):
        n = w.shape[1] // P
        c = w.reshape(KT, P, n, P).transpose(1, 2, 0, 3).reshape(P, n * D)
        return np.concatenate([c, np.zeros((P, CW - c.shape[1]), f32)], 1)

    def by_half(w):
        return list(w.reshape(2, 4, P, 512).transpose(0, 2, 1, 3).reshape(2, P, CW))

    small = np.concatenate([ga, np.zeros((D, 16), f32), ff, np.zeros((D, P - 36), f32)], 1)
    chunks = [by_tile(w) for w in (small, np.concatenate([gq, gk], 1), fq, fk)] + by_half(np.concatenate([fv, gv], 1))
    chunks += [by_tile(w) for w in (mq, mk)] + by_half(np.concatenate([mv, gr], 1))
    g = gt.reshape(D, 3, KT, P).transpose(0, 2, 1, 3).reshape(D, 24, P)
    gate = [by_tile(g[:, 2 * i:2 * i + 2].reshape(D, 256)) for i in range(12)]
    u = w_branch.reshape(3, 2, P, KT // 2, 2, P).transpose(3, 2, 4, 0, 1, 5).reshape(KT // 2, P, 1536)
    u = np.concatenate([u, np.zeros((KT // 2, P, CW - 1536), f32)], 2)
    chunks += gate[0:6] + [u[0]] + gate[6:8] + [u[1]] + gate[8:10] + [u[2]] + gate[10:12] + [u[3]]
    chunks += by_half(w_out[:, 0:512]) + by_half(w_out[:, 512:1024])
    wmix = np.stack(chunks)
    assert wmix.shape == (N_MIX, P, CW)
    gu = np.asarray(w_gu)[0].reshape(E, 4, 2, P, 2, 512, 2)
    dn = np.asarray(w_dn)[0].reshape(E, 4, 2, P, D)
    wexp = np.empty((E, CPE, P, CW), f32)
    wexp[:, 0:8] = gu.transpose(0, 4, 1, 3, 2, 6, 5).reshape(E, 8, P, CW)
    wexp[:, 8:12] = dn.transpose(0, 1, 3, 2, 4).reshape(E, 4, P, CW)
    b1 = np.asarray(b_gu)[0].reshape(E, 2, 512, 2).transpose(0, 1, 3, 2).reshape(E, 2 * D)
    b_moe = np.concatenate([b1, np.asarray(b_dn)[0]], 1)
    cf, cb, masks, extra = constants()
    arrays = {
        "xT": x.T.reshape(KT, P, T).transpose(1, 0, 2), "x": x.reshape(TT, P, D).transpose(1, 0, 2),
        "wmix": wmix, "wexp": wexp.reshape(E * CPE * P, CW),
        "a_up": np.asarray(gla_a_up)[0], "a_b": np.asarray(gla_a_b)[0].reshape(P, 1), "fb": np.asarray(fox_fb)[0].reshape(HEADS, 1),
        "norm_g": np.asarray(gla_norm_g)[0], "ln1_g": np.asarray(ln1_g)[0], "ln1_b": np.asarray(ln1_b)[0],
        "w_router": np.asarray(w_router)[0].reshape(KT, P, E).transpose(1, 0, 2), "b_router": np.asarray(b_router)[0],
        "b_moe": b_moe, "ln2_g": np.asarray(ln2_g)[0], "ln2_b": np.asarray(ln2_b)[0],
        "cf": cf, "cb": cb, "masks": masks, "extra_c": extra,
    }
    arrays = {n: np.ascontiguousarray(a) for n, a in arrays.items()}
    nc = bacc.Bacc("TRN2", target_bir_lowering=False, num_devices=1)
    ins = {n: nc.dram_tensor(f"in_{n}", a.shape, mybir.dt.from_np(a.dtype), kind="ExternalInput").ap()
           for n, a in arrays.items()}
    out = nc.dram_tensor("out", (T, D), mybir.dt.float32, kind="ExternalOutput").ap()
    build_kernel(nc, out=out, **ins)
    r = run_bass_kernel_spmd(nc, [{f"in_{n}": a for n, a in arrays.items()}], core_ids=[0])
    return r.results[0]["out"].reshape(1, T, D)
```
